# Optimizing a Trainium2 kernel written in Bass

```python
import jax, jax.numpy as jnp
from jax import lax
import numpy as np

D_MODEL = 1024
BATCH = 1
SEQ = 1024
DEPTH = 1

ATT_HEADS = 8
ATT_HEAD_DIM = 64
ATT_WIDTH = ATT_HEADS * ATT_HEAD_DIM
Q_BLOCK = 128
CONV_WIDTH = 512
CONV_TAPS = 31
SC_WIDTH = 512
SC_TAPS = 3
N_BRANCH = 3
_IN_SIZES = (ATT_WIDTH, ATT_WIDTH, ATT_WIDTH, ATT_HEADS,
             CONV_WIDTH, CONV_WIDTH, SC_WIDTH, SC_WIDTH, SC_WIDTH)
IN_COLS = sum(_IN_SIZES)
IN_SPLITS = [sum(_IN_SIZES[:i + 1]) for i in range(len(_IN_SIZES) - 1)]
N_EXPERTS = 32
N_GROUPS = 8
EXPERTS_PER_GROUP = N_EXPERTS // N_GROUPS
TOP_K = 2
EXPERT_FF = 512
DISPATCH_BLOCK = 256
DEEPNORM_ALPHA = (2 * DEPTH) ** 0.25
DEEPNORM_BETA = (8 * DEPTH) ** -0.25
LN_EPS = 1e-5

kernel_name = "fox_conformer_shortconv_grouped_moe_deepnorm"

def layer_norm(x, g, b):
    xf = x.astype(jnp.float32)
    mu = jnp.mean(xf, axis=-1, keepdims=True)
    xc = xf - mu
    var = jnp.mean(xc * xc, axis=-1, keepdims=True)
    y = xc * lax.rsqrt(var + LN_EPS) * g.astype(jnp.float32) + b.astype(jnp.float32)
    return y.astype(x.dtype)

def causal_depthwise_conv(x, w):
    taps, chans = w.shape
    return lax.conv_general_dilated(
        x, w[:, None, :].astype(x.dtype), window_strides=(1,),
        padding=((taps - 1, 0),), dimension_numbers=("NWC", "WIO", "NWC"),
        feature_group_count=chans)

def fox_attention(q, k, v, f_logit):
    B, S, H, Dh = q.shape
    scale = Dh ** -0.5
    c = jnp.cumsum(jax.nn.log_sigmoid(f_logit.astype(jnp.float32)), axis=1)
    c = jnp.transpose(c, (0, 2, 1))
    q = jnp.transpose(q, (0, 2, 1, 3))
    k = jnp.transpose(k, (0, 2, 1, 3))
    v = jnp.transpose(v, (0, 2, 1, 3))
    outs = []
    for i in range(S // Q_BLOCK):
        lo, hi = i * Q_BLOCK, (i + 1) * Q_BLOCK
        qb = q[:, :, lo:hi]
        kb = k[:, :, :hi]
        vb = v[:, :, :hi]
        s = jnp.einsum("bhqd,bhkd->bhqk", qb, kb).astype(jnp.float32) * scale
        s = s + c[:, :, lo:hi, None] - c[:, :, None, :hi]
        mask = (lo + jnp.arange(Q_BLOCK))[:, None] >= jnp.arange(hi)[None, :]
        s = jnp.where(mask, s, -jnp.inf)
        p = jax.nn.softmax(s, axis=-1).astype(vb.dtype)
        outs.append(jnp.einsum("bhqk,bhkd->bhqd", p, vb))
    o = jnp.concatenate(outs, axis=2)
    return jnp.transpose(o, (0, 2, 1, 3)).reshape(B, S, H * Dh)

def hybrid_mixer(x, w_in, b_forget, conv_w, conv_b, conv_ln_g, conv_ln_b, sc_w,
                 w_branch, w_gate, b_gate, w_out):
    B, S, _ = x.shape
    z = x @ w_in
    q, k, v, f, glu_a, glu_g, sc_b, sc_c, sc_h = jnp.split(z, IN_SPLITS, axis=-1)
    shp = (B, S, ATT_HEADS, ATT_HEAD_DIM)
    br_att = fox_attention(q.reshape(shp), k.reshape(shp), v.reshape(shp), f + b_forget)
    u = glu_a * jax.nn.sigmoid(glu_g)
    u = causal_depthwise_conv(u, conv_w) + conv_b
    br_conv = jax.nn.silu(layer_norm(u, conv_ln_g, conv_ln_b))
    br_sc = sc_b * causal_depthwise_conv(sc_c * sc_h, sc_w)
    merged = None
    for n, br in enumerate((br_att, br_conv, br_sc)):
        gate = jax.nn.sigmoid(x @ w_gate[n] + b_gate[n])
        term = gate * (br @ w_branch[n])
        merged = term if merged is None else merged + term
    return merged @ w_out

def grouped_moe(x, w_router, b_router, w_up, w_down):
    B, S, D = x.shape
    T = B * S
    M = DISPATCH_BLOCK
    xt = x.reshape(T, D)
    logits = (xt @ w_router).astype(jnp.float32) + b_router.astype(jnp.float32)
    probs = jax.nn.softmax(logits, axis=-1).reshape(T, N_GROUPS, EXPERTS_PER_GROUP)
    vals, idx = lax.top_k(probs, TOP_K)
    best = jnp.argmax(vals.sum(-1), axis=-1)
    sel_vals = jnp.take_along_axis(vals, best[:, None, None], axis=1)[:, 0]
    sel_idx = jnp.take_along_axis(idx, best[:, None, None], axis=1)[:, 0] \
        + best[:, None] * EXPERTS_PER_GROUP
    gates = sel_vals / jnp.sum(sel_vals, axis=-1, keepdims=True)
    A = T * TOP_K
    e_flat = sel_idx.reshape(A).astype(jnp.int32)
    g_flat = gates.reshape(A)
    tok_flat = jnp.arange(A, dtype=jnp.int32) // TOP_K
    order = jnp.argsort(e_flat)
    e_sorted = e_flat[order]
    counts = jnp.bincount(e_flat, length=N_EXPERTS).astype(jnp.int32)
    padded = (counts + M - 1) // M * M
    pad_end = jnp.cumsum(padded)
    pad_start = pad_end - padded
    start = jnp.cumsum(counts) - counts
    dest = pad_start[e_sorted] + jnp.arange(A, dtype=jnp.int32) - start[e_sorted]
    n_blocks = (A + N_EXPERTS * (M - 1) + M - 1) // M
    P = n_blocks * M
    slot_tok = jnp.full((P,), T, jnp.int32).at[dest].set(tok_flat[order])
    slot_gate = jnp.zeros((P,), jnp.float32).at[dest].set(g_flat[order])
    block_expert = jnp.minimum(
        jnp.searchsorted(pad_end, jnp.arange(n_blocks, dtype=jnp.int32) * M, side="right"),
        N_EXPERTS - 1)
    x_pad = jnp.concatenate([xt, jnp.zeros((1, D), xt.dtype)], axis=0)
    xs = x_pad[slot_tok].reshape(n_blocks, M, D)

    def expert_block(args):
        xb, e = args
        a, g = jnp.split(xb @ w_up[e], 2, axis=-1)
        return (jax.nn.silu(g) * a) @ w_down[e]

    ys = lax.map(expert_block, (xs, block_expert)).reshape(P, D)
    out = jax.ops.segment_sum(ys * slot_gate[:, None].astype(ys.dtype), slot_tok,
                              num_segments=T + 1)[:T]
    return out.reshape(B, S, D)

def setup_inputs(seed: int = 0) -> dict:
    key = jax.random.key(seed)
    ks = jax.random.split(key, 24)
    f32 = jnp.float32
    L, D = DEPTH, D_MODEL
    nrm = lambda k, shape: jax.random.normal(k, shape, f32)
    x = nrm(ks[0], (BATCH, SEQ, D))
    w_in = nrm(ks[1], (L, D, IN_COLS)) * D ** -0.5
    b_forget = 3.0 + 0.1 * nrm(ks[2], (L, ATT_HEADS))
    conv_w = nrm(ks[3], (L, CONV_TAPS, CONV_WIDTH)) * CONV_TAPS ** -0.5
    conv_b = 0.02 * nrm(ks[4], (L, CONV_WIDTH))
    conv_ln_g = 1.0 + 0.02 * nrm(ks[5], (L, CONV_WIDTH))
    conv_ln_b = 0.02 * nrm(ks[6], (L, CONV_WIDTH))
    sc_w = nrm(ks[7], (L, SC_TAPS, SC_WIDTH)) * SC_TAPS ** -0.5
    w_branch = nrm(ks[8], (L, N_BRANCH, ATT_WIDTH, D)) * (ATT_WIDTH ** -0.5 * DEEPNORM_BETA)
    w_gate = nrm(ks[9], (L, N_BRANCH, D, D)) * D ** -0.5
    b_gate = 0.02 * nrm(ks[10], (L, N_BRANCH, D))
    w_out = nrm(ks[11], (L, D, D)) * (D ** -0.5 * DEEPNORM_BETA)
    ln1_g = 1.0 + 0.02 * nrm(ks[12], (L, D))
    ln1_b = 0.02 * nrm(ks[13], (L, D))
    w_up = nrm(ks[14], (L, N_EXPERTS, D, 2 * EXPERT_FF)) * D ** -0.5
    w_down = nrm(ks[15], (L, N_EXPERTS, EXPERT_FF, D)) * (EXPERT_FF ** -0.5 * DEEPNORM_BETA)
    ln2_g = 1.0 + 0.02 * nrm(ks[16], (L, D))
    ln2_b = 0.02 * nrm(ks[17], (L, D))
    w_router = nrm(ks[18], (D, N_EXPERTS)) * D ** -0.5
    b_router = 0.01 * nrm(ks[19], (N_EXPERTS,))
    return {"x": x, "w_in": w_in, "b_forget": b_forget, "conv_w": conv_w,
            "conv_b": conv_b, "conv_ln_g": conv_ln_g, "conv_ln_b": conv_ln_b,
            "sc_w": sc_w, "w_branch": w_branch, "w_gate": w_gate, "b_gate": b_gate,
            "w_out": w_out, "ln1_g": ln1_g, "ln1_b": ln1_b, "w_up": w_up,
            "w_down": w_down, "ln2_g": ln2_g, "ln2_b": ln2_b,
            "w_router": w_router, "b_router": b_router}

def reference(x, w_in, b_forget, conv_w, conv_b, conv_ln_g, conv_ln_b, sc_w,
              w_branch, w_gate, b_gate, w_out, ln1_g, ln1_b, w_up, w_down,
              ln2_g, ln2_b, w_router, b_router):
    for l in range(DEPTH):
        h = hybrid_mixer(x, w_in[l], b_forget[l], conv_w[l], conv_b[l], conv_ln_g[l],
                         conv_ln_b[l], sc_w[l], w_branch[l], w_gate[l], b_gate[l], w_out[l])
        x = layer_norm(DEEPNORM_ALPHA * x + h, ln1_g[l], ln1_b[l])
        m = grouped_moe(x, w_router, b_router, w_up[l], w_down[l])
        x = layer_norm(DEEPNORM_ALPHA * x + m, ln2_g[l], ln2_b[l])
    return x


_drawn_inputs = setup_inputs


def setup_inputs(seed=0):
    import zlib

    import numpy as np

    out = dict(_drawn_inputs(seed))
    spreads = {}
    factors = {'b_forget': 34.808,
     'conv_b': 3.859,
     'conv_ln_g': 4.329,
     'conv_ln_b': 7.729,
     'b_gate': 5.446,
     'ln2_g': 8.203,
     'ln2_b': 8.23}
    for name, (base, spread) in spreads.items():
        noise = np.random.default_rng([zlib.crc32(name.encode()), seed]).standard_normal(out[name].shape)
        drawn = base * np.exp(spread * noise) if base else spread * noise
        out[name] = __import__('jax').numpy.asarray(drawn.astype(out[name].dtype))
    for name, factor in factors.items():
        out[name] = (out[name] * factor).astype(out[name].dtype)
    return out
```

```python
import numpy as np
import concourse.bass as bass
from concourse import mybir
from contextlib import ExitStack

FP32 = mybir.dt.float32
FP32R = mybir.dt.float32r
BF16 = mybir.dt.bfloat16
I32 = mybir.dt.int32
ALU = mybir.AluOpType
ACT = mybir.ActivationFunctionType
AX = mybir.AxisListType

P = 128
SEQ = 1024
D = 1024
KT = D // P
TT = SEQ // P
HALF = 512
HEADS, DH = 8, 64
W = 512
CT = W // P
CTAPS, STAPS = 31, 3
NBR = 3
Q0, K0, V0, F0 = 0, W, 2 * W, 3 * W
A0 = F0 + HEADS
G0, B0, C0, H0 = A0 + W, A0 + 2 * W, A0 + 3 * W, A0 + 4 * W
KC = 4
RING = 4
RING5 = 3
ROW_CONVW = 0
ROW_SCW = CTAPS
ROW_CONVB = ROW_SCW + STAPS
ROW_LNG = ROW_CONVB + 1
ROW_LNB = ROW_LNG + 1
ROW_BGATE = ROW_LNB + 1
ROWS = ROW_BGATE + NBR * D // W
NE, NG, EPG, TOPK = 32, 8, 4, 2
FF = 512
NBLK = NE + (SEQ * TOPK) // P
UPT, DNT = D // P, FF // P
XT = UPT + DNT
RRAW, RSPL = 12, 6
ALPHA = 2.0 ** 0.25
EPS = 1e-5
MASKED = -1e30
KB = 1024
PASSES = 3
CONV_LINKS = CTAPS + STAPS
LN_D = 5

KINDS = ("g", "a", "c", "h", "b", "q", "k", "v")
COL = dict(g=G0, a=A0, c=C0, h=H0, b=B0, q=Q0, k=K0, v=V0)
NCH = 2 * len(KINDS)


def program(nc, x, w_in, b_forget, conv_w, conv_b, conv_ln_g, conv_ln_b, sc_w,
            w_branch, w_gate, b_gate, w_out, ln1_g, ln1_b, w_up, w_down,
            ln2_g, ln2_b, w_router, b_router, out):
    ctx = ExitStack()
    base = (nc.sbuf_base + 127) // 128 * 128

    def at(name, shape, dtype, kb):
        return nc.alloc_sbuf_tensor_at(name, shape, dtype, offset=base + int(kb * KB))

    def sem(name):
        return ctx.enter_context(nc.semaphore(name))

    with ctx:
        ctx.enter_context(nc.sbuf_tensor("whole_map", [P, 207 * KB // 4], FP32))
        xt_hi = at("xt_hi", [P, KT, SEQ], FP32R, 0)
        xt_lo = at("xt_lo", [P, KT, SEQ], FP32R, 32)
        x_raw = at("x_raw", [P, TT, D], FP32, 64)
        qkv = at("qkv", [P, 3 * CT, SEQ], FP32, 64)
        conv = at("conv", [P, CT, SEQ], FP32, 112)
        sc = at("sc", [P, CT, SEQ], FP32, 128)
        w_raw = at("w_raw", [P, RING, KC, P], FP32, 144)
        w_hi = at("w_hi", [P, RING, KC, P], FP32R, 152)
        w_lo = at("w_lo", [P, RING, KC, P], FP32R, 160)
        upad = at("upad", [P, CTAPS - 1 + SEQ], FP32, 168)
        sg = at("sg", [P, SEQ], FP32, 173)
        hpad = at("hpad", [P, STAPS - 1 + SEQ], FP32, 177)
        cbuf = at("cbuf", [P, SEQ], FP32, 182)
        scacc = at("scacc", [P, SEQ], FP32, 182)
        fz = at("fz", [HEADS, SEQ], FP32, 187)
        fe = at("fe", [HEADS, SEQ], FP32, 191)
        fc = at("fc", [HEADS, SEQ], FP32, 195)
        rows = at("rows", [ROWS, W], FP32, 199)
        wf_raw = at("wf_raw", [P, KT, HEADS], FP32, 201)
        wf_hi = at("wf_hi", [P, KT, HEADS], FP32R, 201.5)
        wf_lo = at("wf_lo", [P, KT, HEADS], FP32R, 202)
        yln = at("yln", [P, 2, W], FP32, 168)
        stat3 = at("stat3", [P, TT, 8], FP32, 172)
        aggr3 = at("aggr3", [P, TT, 2], FP32, 172.5)
        rstd3 = at("rstd3", [P, TT], FP32, 172.75)
        ident = at("ident", [P, P], FP32, 204)
        ident_b = at("ident_b", [P, P], BF16, 204.5)
        mask_b = at("mask_b", [P, 2 * P], BF16, 204.75)
        cols = at("cols", [P, ROWS, CT], FP32, 205.25)
        bf = at("bf", [HEADS, 1], FP32, 206)
        stat = at("stat", [P, 2, 16], FP32, 206.125)
        eps = at("eps", [P, 1], FP32, 206.0625)
        rmax = at("rmax", [P, 2], FP32, 206.25)
        rsum = at("rsum", [P, 2], FP32, 206.3125)
        rinv = at("rinv", [P, 2], FP32, 206.375)
        AUG = DH + 2
        qk_raw = at("qk_raw", [AUG, 2, SEQ], FP32, 144)
        vt_raw = at("vt_raw", [P, SEQ], FP32, 152)
        qk_hi = at("qk_hi", [AUG, 2, SEQ], FP32R, 156)
        qk_lo = at("qk_lo", [AUG, 2, SEQ], FP32R, 164)
        v_hi = at("v_hi", [P, TT, P], FP32R, 172)
        v_lo = at("v_lo", [P, TT, P], FP32R, 176)
        prob = at("prob", [P, 2, SEQ], FP32, 180)
        pt_hi = at("pt_hi", [P, TT, 2 * P], FP32R, 188)
        pt_lo = at("pt_lo", [P, TT, 2 * P], FP32R, 196)
        merged = at("merged", [P, KT, SEQ], FP32, 80)
        br_hi = at("br_hi", [P, CT, SEQ], FP32R, 168)
        br_lo = at("br_lo", [P, CT, SEQ], FP32R, 184)
        gate_s = at("gate_s", [P, SEQ], FP32, 200)
        wo_raw = at("wo_raw", [P, 4, D], FP32, 64)
        wo_hi = at("wo_hi", [P, KT, D], FP32R, 0)
        wo_lo = at("wo_lo", [P, KT, D], FP32R, 32)
        ms_hi = at("ms_hi", [P, KT, P], FP32R, 112)
        ms_lo = at("ms_lo", [P, KT, P], FP32R, 116)
        x_res = at("x_res", [P, D], FP32, 120)
        y1 = at("y1", [P, D], FP32, 124)
        x1 = at("x1", [P, D], FP32, 128)
        x1t = at("x1t", [P, KT, P], FP32, 132)
        lng1 = at("lng1", [P, D], FP32, 136)
        lnb1 = at("lnb1", [P, D], FP32, 140)
        w_rt = at("w_rt", [P, KT, NE], FP32, 144)
        b_rt = at("b_rt", [P, NE], FP32, 145)
        logits = at("logits", [P, TT, NE], FP32, 146)
        prb = at("prb", [P, TT, NE], FP32, 147)
        p2 = at("p2", [P, TT, NE], FP32, 148)
        oh1 = at("oh1", [P, TT, NE], FP32, 149)
        oh2 = at("oh2", [P, TT, NE], FP32, 150)
        rt_t = at("rt_t", [P, TT, NE], FP32, 151)
        rt_u = at("rt_u", [P, TT, NE], FP32, 152)
        sel_b = at("sel_b", [P, TT, NE], BF16, 153)
        kneg = at("kneg", [P, TT, NG, EPG], FP32, 154)
        gneg = at("gneg", [P, TT, NG], FP32, 155)
        thr = at("thr", [P, NE, TT - 1], FP32, 156)
        tri_b = at("tri_b", [P, P], BF16, 157)
        one_b = at("one_b", [P, P], BF16, 157.25)
        dest = at("dest", [P, TT, NE], FP32, 158)
        tcum = at("tcum", [P, TT, NE], FP32, 159)
        gt = at("gt", [P, NE, TT - 1], FP32, 160)
        grp = at("grp", [P, 8, TT, NG], FP32, 161)
        ev = at("ev", [P, 8, NE], FP32, 164)
        biota = at("biota", [P, NBLK], FP32, 165)
        bmap = at("bmap", [P, NBLK, NE], FP32, 166)
        byt = at("byt", [P, 8, TT], FP32, 172.5)
        zeros_i = at("zeros_i", [P, (NBLK + 1) * 2], I32, 173)
        ones_e = at("ones_e", [P, NE], FP32, 174)
        dest_i = at("dest_i", [P, TOPK, TT], I32, 203)
        pairs = at("pairs", [P, TOPK, TT, 2], I32, 203.125)
        expert_i = at("expert_i", [P, NBLK], I32, 203.375)
        last_i = at("last_i", [P, 1], I32, 203.625)
        e_raw = at("e_raw", [P, RRAW, D], FP32, 0)
        e_hi = at("e_hi", [P, RSPL, D], FP32R, 48)
        e_lo = at("e_lo", [P, RSPL, D], FP32R, 72)
        xg = at("xg", [P, D], FP32, 96)
        xe_hi = at("xe_hi", [P, KT, P], FP32R, 100)
        xe_lo = at("xe_lo", [P, KT, P], FP32R, 104)
        sil = at("sil", [P, FF], FP32, 108)
        hid = at("hid", [P, FF], FP32, 110)
        ht_hi = at("ht_hi", [P, DNT, P], FP32R, 112)
        ht_lo = at("ht_lo", [P, DNT, P], FP32R, 114)
        ye = at("ye", [P, D], FP32, 116)
        slots = at("slots", [P, NBLK + 1, 2], I32, 120)
        tok_i = at("tok_i", [P, 1], I32, 120.5)
        comb = at("comb", [P, TT, D], FP32, 140)
        zout = at("zout", [P, 2, D], FP32, 124)
        lng2 = at("lng2", [P, D], FP32, 132)
        lnb2 = at("lnb2", [P, D], FP32, 136)

        ps = ctx.enter_context(nc.psum_tensor("ps", [P, 8, HALF], FP32))

        forget_d = nc.dram_tensor("forget_d", [HEADS, 2, 2, SEQ], FP32, kind="Internal").ap()
        x1_d = nc.dram_tensor("x1_d", [SEQ, D], FP32, kind="Internal").ap()
        slot_d = nc.dram_tensor("slot_d", [(NBLK + 1) * P, 2], I32, kind="Internal").ap()
        y_d = nc.dram_tensor("y_d", [NBLK * P, D], FP32, kind="Internal").ap()

        x_in, rows_in, wf_in, forget_out = sem("x_in"), sem("rows_in"), sem("wf_in"), sem("forget_out")
        consts, pads, xt_t, xt_h, xt_l = sem("consts"), sem("pads"), sem("xt_t"), sem("xt_h"), sem("xt_l")
        cols_t, cols_ok, wf_h, wf_l, f_mm, f_act, f_dve = (sem(n) for n in (
            "cols_t", "cols_ok", "wf_h", "wf_l", "f_mm", "f_act", "f_dve"))
        raw_in = [sem(f"raw_in{i}") for i in range(RING)]
        hi_ok = sem("hi_ok")
        fill_out = sem("fill_out")
        lo_ok = sem("lo_ok")
        w_used = sem("w_used")
        evac = [sem("evac0"), sem("evac1")]
        conv_chain = sem("conv_chain")
        ln_stats = sem("ln_stats")
        ln_t, ln_dve, ln_t2, ln_act = sem("ln_t"), sem("ln_dve"), sem("ln_t2"), sem("ln_act")
        qk_in, v_in = sem("qk_in"), sem("v_in")
        qk_h, qk_l = sem("qk_h"), sem("qk_l")
        v_t, v_h, v_l = sem("v_t"), sem("v_h"), sem("v_l")
        s_ok, max_ok, exp_ok, inv_ok, norm_ok = sem("s_ok"), sem("max_ok"), sem("exp_ok"), sem("inv_ok"), sem("norm_ok")
        t_ok, pt_h, pt_l, o_ok, o_out = sem("t_ok"), sem("pt_h"), sem("pt_l"), sem("o_ok"), sem("o_out")
        raw5_in = [sem(f"raw5_in{i}") for i in range(RING5)]
        hi5, lo5, used5 = sem("hi5"), sem("lo5"), sem("used5")
        br_h, br_l, gate_ok, merge_ok, merge_chain = sem("br_h"), sem("br_l"), sem("gate_ok"), sem("merge_ok"), sem("merge_chain")
        wo_in = [sem(f"wo_in{i}") for i in range(4)]
        wo_h, wo_l, par6_in, xres_in = sem("wo_h"), sem("wo_l"), sem("par6_in"), sem("xres_in")
        ms_h, ms_l, y_mm, y1_ok, ln6, z6, g6, x1_ok, x1_out = (sem(n) for n in (
            "ms_h", "ms_l", "y_mm", "y1_ok", "ln6", "z6", "g6", "x1_ok", "x1_out"))
        rt_t1, rt_c, rt_mm, lg_ok = sem("rt_t1"), sem("rt_c"), sem("rt_mm"), sem("lg_ok")
        r_const, r_chain, r_exp, r_sel, r_cnt, r_done, zero_out, scat, scat_all = (sem(n) for n in (
            "r_const", "r_chain", "r_exp", "r_sel", "r_cnt", "r_done", "zero_out", "scat", "scat_all"))
        eraw_in = [sem(f"eraw_in{i}") for i in range(RRAW)]
        e_h, e_l, e_used = sem("e_h"), sem("e_l"), sem("e_used")
        slot_in, tok_ok, xg_in = sem("slot_in"), sem("tok_ok"), sem("xg_in")
        tx_ok, xe_h, xe_l, sil_ok, hid_ok = sem("tx_ok"), sem("xe_h"), sem("xe_l"), sem("sil_ok"), sem("hid_ok")
        th_ok, ht_h, ht_l, ye_ok, ye_out = sem("th_ok"), sem("ht_h"), sem("ht_l"), sem("ye_ok"), sem("ye_out")
        par9_in, comb_in, comb_s = sem("par9_in"), sem("comb_in"), sem("comb_s")
        add1 = [sem(f"add1_{t}") for t in range(TT)]
        add2 = [sem(f"add2_{t}") for t in range(TT)]
        ln9, z9, g9, out_ok, out_dma = sem("ln9"), sem("z9"), sem("g9"), sem("out_ok"), [sem("out_dma0"), sem("out_dma1")]

        std3, std6, std9 = sem("std3"), sem("std6"), sem("std9")

        passed_sp, passed_pool, passed_dve = sem("passed_sp"), sem("passed_pool"), sem("passed_dve")

        block = ctx.enter_context(nc.Block())

        def flat(b, n=2):
            return ps[:, b:b + n, :].rearrange("p a b -> p (a b)")

        def tiles(b, n=2):
            return ps[:, b:b + n, :].rearrange("p a (k n) -> p (a k) n", n=P)

        def bank3(t):
            return (t + 4) % TT

        def nkeys(r):
            return 2 * (r // 2) + 2

        @block.sync
        def _(sp):
            for t in range(TT):
                sp.dma_start(x_raw[:, t, :], x[0, t * P:(t + 1) * P, :]).then_inc(x_in, 16)
            for lo, hi, src in ((ROW_CONVW, ROW_SCW, conv_w[0]), (ROW_SCW, ROW_CONVB, sc_w[0]), (ROW_CONVB, ROW_LNG, conv_b),
                                (ROW_LNG, ROW_LNB, conv_ln_g), (ROW_LNB, ROW_BGATE, conv_ln_b),
                                (ROW_BGATE, ROWS, b_gate[0].rearrange("n (h w) -> (n h) w", w=W))):
                sp.dma_start(rows[lo:hi, :], src).then_inc(rows_in, 16)
            sp.dma_start(wf_raw[:], w_in[0, :, F0:A0].rearrange("(k p) n -> p k n", p=P),
                         allow_slow_non_contiguous=True).then_inc(wf_in, 16)
            sp.dma_start(bf[:], b_forget.rearrange("a h -> h a"), allow_slow_non_contiguous=True).then_inc(wf_in, 16)
            with nc.sync.Fori(0, CT) as i:
                for c in range(NCH):
                    kind, half = KINDS[c // 2], c % 2
                    src = w_in[0, half * KC * P:(half + 1) * KC * P, bass.ds(i * P + COL[kind], P)]
                    sp.wait_ge(lo_ok, i * NCH + c + 1)
                    sp.sem_inc(passed_sp, 1)
                    sp.dma_start(w_raw[:, c % RING], src.rearrange("(k p) n -> p k n", p=P)).then_inc(raw_in[c % RING], 16)
            sp.wait_ge(ln_act, TT)
            sp.wait_ge(evac[1], 1 + CT * len(KINDS) // 2)
            sp.wait_ge(forget_out, 64)
            with nc.sync.Fori(0, HEADS // 2) as i:
                sp.wait_ge(v_l, i + 1)
                sp.dma_start(vt_raw[:], qkv[:, bass.ds(2 * CT + i, 1), :].rearrange("p a n -> p (a n)")).then_inc(v_in, 16)
                for u in range(2):
                    sp.wait_ge(qk_l, 2 * i + u + 1)
                    for s in range(2):
                        sp.dma_start(qk_raw[0:DH, s, :], qkv[u * DH:(u + 1) * DH, bass.ds(s * CT + i, 1), :].rearrange("p a n -> p (a n)")).then_inc(qk_in, 16)
                    sp.dma_start(qk_raw[DH:AUG, :, :], forget_d[bass.ds(2 * i + u, 1)].rearrange("a s r n -> (a r) s n")).then_inc(qk_in, 16)
            sp.wait_ge(o_out, HEADS * TT // 2 + 1)
            for n in range(NBR):
                with nc.sync.Fori(0, KT) as i:
                    for c in range(RING5):
                        sp.wait_ge(lo5, (n * KT + i) * RING5 + c + 1)
                        if c < 2:
                            src = w_gate[0, n, c * KC * P:(c + 1) * KC * P, bass.ds(i * P, P)]
                        else:
                            src = w_branch[0, n, :, bass.ds(i * P, P)]
                        sp.dma_start(w_raw[:, c], src.rearrange("(k p) n -> p k n", p=P)).then_inc(raw5_in[c], 16)
                if n == 0:
                    sp.wait_ge(br_l, 1)
                    for k in range(4):
                        sp.dma_start(wo_raw[:, k, :], w_out[0, k * P:(k + 1) * P, :]).then_inc(wo_in[k], 16)
            for k in range(4, KT):
                sp.wait_ge(wo_l, k - 3)
                sp.dma_start(wo_raw[:, k % 4, :], w_out[0, k * P:(k + 1) * P, :]).then_inc(wo_in[k % 4], 16)
            sp.wait_ge(merge_ok, NBR * KT + 1)
            sp.dma_start(w_rt[:], w_router.rearrange("(k p) n -> p k n", p=P)).then_inc(par6_in, 16)
            sp.dma_start(b_rt[:], b_router.partition_broadcast(P)).then_inc(par6_in, 16)
            sp.dma_start(lng1[:], ln1_g[0].partition_broadcast(P)).then_inc(par6_in, 16)
            sp.dma_start(lnb1[:], ln1_b[0].partition_broadcast(P)).then_inc(par6_in, 16)
            with nc.sync.Fori(0, TT) as t:
                sp.wait_ge(y1_ok, t + 1)
                sp.dma_start(x_res[:], x[0, bass.ds(t * P, P), :]).then_inc(xres_in, 16)
                sp.wait_ge(x1_ok, t + 1)
                sp.dma_start(x1_d[bass.ds(t * P, P), :], x1[:]).then_inc(x1_out, 16)
            def load(n, s0, src):
                sp.wait_ge(e_l, n + 1)
                sp.dma_start(e_raw[:, s0 % RRAW, :], src).then_inc(eraw_in[s0 % RRAW], 16)

            sp.wait_ge(y_mm, TT)
            for s in range(UPT):
                load(s, s, w_up[0, 0, s * P:(s + 1) * P, :])
            sp.wait_ge(r_done, 1)
            sp.wait_ge(scat_all, 1)
            sp.dma_start(lng2[:], ln2_g[0].partition_broadcast(P)).then_inc(par9_in, 16)
            sp.dma_start(lnb2[:], ln2_b[0].partition_broadcast(P)).then_inc(par9_in, 16)
            sp.wait_ge(x1_out, 16 * TT)
            sp.dma_start(comb[:], x1_d.rearrange("(t p) n -> p t n", p=P)).then_inc(comb_in, 16)

            last_b = nc.sync.value_load(last_i[0:1, 0:1], min_val=NE - 1, max_val=NBLK - 1)
            with nc.sync.Fori(1, last_b + 1) as b:
                up_e = nc.sync.value_load(expert_i[0:1, bass.ds(b, 1)], min_val=0, max_val=NE - 1)
                dn_e = nc.sync.value_load(expert_i[0:1, bass.ds(b - 1, 1)], min_val=0, max_val=NE - 1)
                for s in range(XT):
                    n = UPT + (b - 1) * XT + s
                    if s < UPT:
                        src = w_up[0, bass.ds(up_e, 1), s * P:(s + 1) * P, :]
                    else:
                        src = w_down[0, bass.ds(dn_e, 1), (s - UPT) * P:(s - UPT + 1) * P, :]
                    load(n, UPT + s, src.rearrange("a p n -> (a p) n"))
            last_e = nc.sync.value_load(expert_i[0:1, bass.ds(last_b, 1)], min_val=0, max_val=NE - 1)
            for s in range(DNT):
                src = w_down[0, bass.ds(last_e, 1), s * P:(s + 1) * P, :]
                load(UPT + last_b * XT + s, UPT + s, src.rearrange("a p n -> (a p) n"))
            for t in range(TT):
                sp.wait_ge(out_ok, t + 1)
                sp.dma_start(out[0, t * P:(t + 1) * P, :], zout[:, t % 2, :]).then_inc(out_dma[t % 2], 16)
            for u in range(2):
                sp.wait_ge(out_dma[u], 16 * TT // 2)

        @block.gpsimd
        def _(pool):
            nc.gpsimd.memset(ident[:], 0.0).then_inc(consts, 1)
            nc.gpsimd.memset(mask_b[:, 0:P], 0.0).then_inc(consts, 1)
            nc.gpsimd.memset(mask_b[:, P:2 * P], MASKED).then_inc(consts, 1)
            pool.wait_ge(consts, 3)
            nc.gpsimd.affine_select(out=ident[:], in_=ident[:], compare_op=ALU.not_equal, fill=1.0,
                                    base=0, pattern=[[-1, P]], channel_multiplier=1).then_inc(consts, 1)
            nc.gpsimd.affine_select(out=mask_b[:, 0:P], in_=mask_b[:, 0:P], compare_op=ALU.is_ge, fill=MASKED,
                                    base=0, pattern=[[-1, P]], channel_multiplier=1).then_inc(consts, 1)
            pool.wait_ge(consts, 5)
            nc.gpsimd.tensor_copy(ident_b[:], ident[:]).then_inc(consts, 1)
            nc.gpsimd.memset(eps[:], EPS).then_inc(consts, 1)
            nc.gpsimd.memset(upad[:, 0:CTAPS - 1], 0.0).then_inc(pads, 1)
            nc.gpsimd.memset(hpad[:, 0:STAPS - 1], 0.0).then_inc(pads, 1)
            pool.wait_ge(f_dve, 4)
            for side, row, src in ((0, 0, fc), (0, 1, fe), (1, 0, fe), (1, 1, fz)):
                pool.dma_start(forget_d[:, side, row, :], src[:]).then_inc(forget_out, 16)
            fill_rows = (NBLK - NE) * P // CT
            with nc.gpsimd.Fori(0, CT) as i:
                pool.wait_ge(w_used, i * NCH + 1 + RING)
                pool.sem_inc(passed_pool, 1)
                pool.dma_start(y_d[bass.ds(i * fill_rows + NE * P, fill_rows), :], x[0, 0:fill_rows, :]).then_inc(fill_out, 16)
            with nc.gpsimd.Fori(0, HEADS // 2) as i:
                for g in range(2 * TT):
                    r, n = g % TT, i * 2 * TT + g
                    pool.wait_ge(inv_ok, n + 1)
                    pool.sem_inc(passed_pool, 1)
                    cut = prob[:, g % 2, 0:nkeys(r) * P]
                    nc.gpsimd.tensor_scalar(cut, cut, rinv[:, g % 2:g % 2 + 1], None, ALU.mult).then_inc(norm_ok, 1)
            pool.wait_ge(merge_ok, NBR * KT + 1)
            nc.gpsimd.iota(kneg[:], [[0, TT], [0, NG], [-1, EPG]], base=EPG, channel_multiplier=0,
                           allow_small_or_imprecise_dtypes=True).then_inc(r_const, 1)
            nc.gpsimd.iota(gneg[:], [[0, TT], [-1, NG]], base=NG, channel_multiplier=0,
                           allow_small_or_imprecise_dtypes=True).then_inc(r_const, 1)
            nc.gpsimd.iota(thr[:], [[0, NE], [P, TT - 1]], base=P, channel_multiplier=0,
                           allow_small_or_imprecise_dtypes=True).then_inc(r_const, 1)
            nc.gpsimd.iota(biota[:], [[1, NBLK]], base=0, channel_multiplier=0,
                           allow_small_or_imprecise_dtypes=True).then_inc(r_const, 1)
            for k in range(TOPK):
                nc.gpsimd.iota(pairs[:, k, :, 0:1].rearrange("p t a -> p (t a)"), [[P, TT]], base=0,
                               channel_multiplier=1).then_inc(r_const, 1)
            nc.gpsimd.memset(one_b[:], 1.0).then_inc(r_const, 1)
            nc.gpsimd.memset(ones_e[:], 1.0).then_inc(r_const, 1)
            nc.gpsimd.memset(zeros_i[:], 0).then_inc(r_const, 1)
            pool.wait_ge(r_const, 9)
            nc.gpsimd.affine_select(out=tri_b[:], in_=one_b[:], compare_op=ALU.is_ge, fill=0.0,
                                    base=-1, pattern=[[1, P]], channel_multiplier=-1).then_inc(r_const, 1)
            pool.dma_start(slot_d.rearrange("(p a) b -> p (a b)", p=P), zeros_i[:]).then_inc(zero_out, 16)
            pool.wait_ge(zero_out, 16)
            pool.wait_ge(r_done, 1)
            for t in range(TT):
                for k in range(TOPK):
                    nc.gpsimd.indirect_dma_start(
                        out=slot_d, out_offset=bass.IndirectOffsetOnAxis(ap=dest_i[:, k, t:t + 1], axis=0),
                        in_=pairs[:, k, t, :], in_offset=None).then_inc(scat, 16)
            pool.wait_ge(scat, 16 * TT * TOPK)
            pool.sem_inc(scat_all, 1)
            pool.wait_ge(x1_out, 16 * TT)
            last_b = nc.gpsimd.value_load(last_i[0:1, 0:1], min_val=NE - 1, max_val=NBLK - 1)
            pool.wait_ge(comb_in, 16)
            nc.gpsimd.tensor_scalar(comb[:], comb[:], ALPHA, None, ALU.mult).then_inc(comb_s, 1)
            def gather(b):
                pool.dma_start(slots[:, bass.ds(b, 1), :].rearrange("p a k -> p (a k)"),
                               slot_d[bass.ds(b * P, P), :]).then_inc(slot_in, 16)
                pool.wait_ge(slot_in, 16 * (b + 1))
                pool.sem_inc(passed_pool, 1)
                nc.gpsimd.tensor_copy(tok_i[:], slots[:, bass.ds(b, 1), 0:1].rearrange("p a k -> p (a k)")).then_inc(tok_ok, 1)
                pool.wait_ge(tok_ok, b + 1)
                pool.wait_ge(tx_ok, b + 1)
                pool.sem_inc(passed_pool, 1)
                nc.gpsimd.indirect_dma_start(out=xg[:], out_offset=None, in_=x1_d,
                                             in_offset=bass.IndirectOffsetOnAxis(ap=tok_i[:], axis=0)).then_inc(xg_in, 16)

            gather(0)
            with nc.gpsimd.Fori(1, last_b + 2) as b:
                pool.wait_ge(xg_in, 16 * b)
                gather(b)
            pool.wait_ge(comb_s, 1)
            pool.wait_ge(ye_out, 16 * last_b + 32)
            pool.sem_inc(passed_pool, 1)
            for t in range(TT):
                nc.gpsimd.indirect_dma_start(
                    out=comb[:, t, :], out_offset=None, in_=y_d,
                    in_offset=bass.IndirectOffsetOnAxis(ap=dest_i[:, 0, t:t + 1], axis=0), compute_op=ALU.add).then_inc(add1[t], 16)
            for t in range(TT):
                pool.wait_ge(add1[t], 16)
                nc.gpsimd.indirect_dma_start(
                    out=comb[:, t, :], out_offset=None, in_=y_d,
                    in_offset=bass.IndirectOffsetOnAxis(ap=dest_i[:, 1, t:t + 1], axis=0), compute_op=ALU.add).then_inc(add2[t], 16)

        @block.tensor
        def _(pe):
            def product(o, terms, nk, cut, start, stop):
                for k in nk:
                    for n, (st, mv) in enumerate(terms):
                        for h, c0, c1 in cut:
                            last = nc.tensor.matmul(o(h, c1 - c0), st(k), mv(k, c0, c1),
                                                    start=start and k == nk[0] and n == 0,
                                                    stop=h in stop and k == nk[-1] and n == PASSES - 1)
                return last

            HALVES = ((0, 0, HALF), (1, HALF, 2 * HALF))
            pe.sem_inc(w_used, RING)
            pe.sem_inc(used5, RING5)
            pe.sem_inc(e_used, RSPL)
            pe.sem_inc(tx_ok, 1)
            pe.wait_ge(consts, 6)
            pe.wait_ge(x_in, 16 * TT)
            for t in range(TT):
                if t >= 2:
                    pe.wait_ge(xt_l, t - 1)
                for k in range(KT):
                    last = nc.tensor.transpose(tiles((t % 2) * 2)[:, k, :], x_raw[:, t, k * P:(k + 1) * P], ident[:])
                last.then_inc(xt_t, 1)
            pe.wait_ge(rows_in, 16 * 6)
            for j in range(CT):
                last = nc.tensor.transpose(ps[:, 4, j * ROWS:(j + 1) * ROWS], rows[:, j * P:(j + 1) * P], ident[0:ROWS, 0:ROWS])
            last.then_inc(cols_t, 1)
            pe.wait_ge(xt_l, TT)
            pe.wait_ge(wf_l, 1)
            product(lambda h, n: ps[0:HEADS, 6 + h, :],
                    [(lambda k, w=w: w[:, k, :], lambda k, a, b, v=v: v[:, k, a:b]) for w, v in ((wf_hi, xt_hi), (wf_hi, xt_lo), (wf_lo, xt_hi))],
                    range(KT), HALVES, True, (0, 1)).then_inc(f_mm, 1)
            with nc.tensor.Fori(0, CT) as i:
                for c in range(NCH):
                    tile, half = c // 2, c % 2
                    if half == 0:
                        pe.wait_ge(evac[tile % 2], i * (len(KINDS) // 2) + tile // 2 + 1)
                    pe.wait_ge(lo_ok, i * NCH + c + 1 + RING)
                    product(lambda h, n: ps[:, 2 * (tile % 2) + h, :],
                            [(lambda k, w=w: w[:, c % RING, k - half * KC, :], lambda k, a, b, v=v: v[:, k, a:b])
                             for w, v in ((w_hi, xt_hi), (w_hi, xt_lo), (w_lo, xt_hi))],
                            range(half * KC, (half + 1) * KC), HALVES, half == 0, (0, 1) if half else ()).then_inc(w_used, 1)
            pe.wait_ge(conv_chain, CT * CONV_LINKS)
            for t in range(TT):
                if bank3(t) == 0:
                    pe.wait_ge(evac[0], 1 + CT * len(KINDS) // 2)
                    pe.wait_ge(evac[1], 1 + CT * len(KINDS) // 2)
                for j in range(CT):
                    last = nc.tensor.transpose(ps[:, bank3(t), j * P:(j + 1) * P], conv[:, j, t * P:(t + 1) * P], ident[:])
                last.then_inc(ln_t, 1)
            for t in range(TT):
                pe.wait_ge(ln_dve, t + 2)
                for j in range(CT):
                    last = nc.tensor.transpose(ps[:, bank3(t), j * P:(j + 1) * P], yln[:, t % 2, j * P:(j + 1) * P], ident[:])
                last.then_inc(ln_t2, 1)
            with nc.tensor.Fori(0, HEADS // 2) as i:
                pe.wait_ge(v_in, 16 * (i + 1))
                pe.wait_ge(pt_l, i * 2 * TT + 1)
                for k in range(TT):
                    last = nc.tensor.transpose(tiles(4)[:, k, :], vt_raw[:, k * P:(k + 1) * P], ident[:])
                last.then_inc(v_t, 1)
                for g in range(2 * TT + 3):
                    if g < 2 * TT:
                        u, r = g // TT, g % TT
                        nk = nkeys(r) * P
                        if r == 0:
                            pe.wait_ge(qk_l, 2 * i + u + 2)
                        if g >= 2:
                            pe.wait_ge(exp_ok, i * 2 * TT + g - 1)
                        elif g == 0:
                            pe.wait_ge(o_out, i * TT + 1)
                        b = 2 * (g % 2)
                        m0 = r * P
                        cut = [(h, a, min(a + HALF, nk)) for h, a in enumerate(range(0, nk, HALF))]
                        product(lambda h, n: ps[:, b + h, 0:n],
                                [(lambda k, q=q: q[:, 0, r * P:(r + 1) * P], lambda k, a, e, v=v: v[:, 1, a:e])
                                 for q, v in ((qk_hi, qk_hi), (qk_hi, qk_lo), (qk_lo, qk_hi))],
                                [0], cut, True, [h for h, _, _ in cut if h != m0 // HALF])
                        nc.tensor.matmul(flat(b)[:, m0:nk], ident_b[:], mask_b[:, 0:nk - m0],
                                         start=False, stop=True).then_inc(s_ok, 1)
                    t = g - 2
                    if t >= 0:
                        if t % 2 == 0 and t >= 2:
                            pe.wait_ge(pt_l, i * 2 * TT + t + 1)
                            pe.wait_ge(o_out, i * TT + (t - 2) // 2 + 1)
                            last_r = (t - 1) % TT
                            for k in range(nkeys(last_r)):
                                for n, (v, p) in enumerate(((v_hi, pt_hi), (v_hi, pt_lo), (v_lo, pt_hi))):
                                    last = nc.tensor.matmul(ps[:, 6, 0:2 * P], v[:, k, :], p[:, k, :],
                                                            start=k == 0 and n == 0, stop=k == nkeys(last_r) - 1 and n == PASSES - 1)
                            last.then_inc(o_ok, 1)
                        if t < 2 * TT:
                            pe.wait_ge(norm_ok, i * 2 * TT + t + 1)
                            if t == 0:
                                pe.wait_ge(v_l, i + 2)
                            else:
                                pe.wait_ge(pt_l, i * 2 * TT + t + 1)
                            for k in range(nkeys(t % TT)):
                                last = nc.tensor.transpose(tiles(4)[:, k, :], prob[:, t % 2, k * P:(k + 1) * P], ident[:])
                            last.then_inc(t_ok, 1)
            for m in range(NBR):
                with nc.tensor.Fori(0, KT) as i:
                    for c in range(RING5):
                        pe.wait_ge(lo5, (m * KT + i) * RING5 + c + 1 + RING5)
                        if c == 0:
                            pe.wait_ge(gate_ok, m * KT + i + 1)
                        if c == 2:
                            pe.wait_ge(br_l, m + 1)
                            pe.wait_ge(merge_ok, m * KT + i + 1)
                        mh, ml = (xt_hi, xt_lo) if c < 2 else (br_hi, br_lo)
                        k0 = KC * c if c < 2 else 0
                        product(lambda h, n: ps[:, (0 if c < 2 else 2) + h, :],
                                [(lambda k, w=w: w[:, c, k - k0, :], lambda k, a, b, v=v: v[:, k, a:b])
                                 for w, v in ((w_hi, mh), (w_hi, ml), (w_lo, mh))],
                                range(k0, k0 + KC), HALVES, c != 1, (0, 1) if c else ()).then_inc(used5, 1)

            def project(t):
                pe.wait_ge(ms_l, t + 1)
                pe.wait_ge(y1_ok, t + 1)
                product(lambda h, n: ps[:, h, :],
                        [(lambda k, s=s: s[:, k, :], lambda k, a, b, v=v: v[:, k, a:b]) for s, v in ((ms_hi, wo_hi), (ms_hi, wo_lo), (ms_lo, wo_hi))],
                        range(KT), HALVES, True, (0, 1)).then_inc(y_mm, 1)

            def route(t):
                pe.wait_ge(x1_ok, t + 1)
                pe.wait_ge(rt_c, t + 1)
                for k in range(KT):
                    last = nc.tensor.transpose(tiles(4)[:, k, :], x1[:, k * P:(k + 1) * P], ident[:])
                last.then_inc(rt_t1, 1)
                pe.wait_ge(rt_c, t + 2)
                pe.wait_ge(lg_ok, t + 1)
                for k in range(KT):
                    last = nc.tensor.matmul(ps[:, 6, 0:NE], x1t[:, k, :], w_rt[:, k, :], start=k == 0, stop=k == KT - 1)
                last.then_inc(rt_mm, 1)

            pe.wait_ge(wo_l, KT)
            pe.wait_ge(merge_ok, NBR * KT + 1)
            pe.wait_ge(par6_in, 64)
            project(0)
            with nc.tensor.Fori(1, TT) as t:
                project(t)
                route(t - 1)
            route(TT - 1)
            pe.wait_ge(r_sel, 1)
            pe.wait_ge(r_const, 10)
            selv = sel_b[:].rearrange("p t e -> p (t e)")
            nc.tensor.matmul(ps[:, 0, 0:TT * NE], tri_b[:], selv, start=True, stop=True)
            nc.tensor.matmul(ps[:, 1, 0:TT * NE], one_b[:], selv, start=True, stop=True).then_inc(r_cnt, 1)

            def weights(n, s0, stat, s, banks, nk):
                pe.wait_ge(e_l, n + 1 + RRAW)
                sh, sl = stat
                for m, (st, w) in enumerate(((sh, e_hi), (sh, e_lo), (sl, e_hi))):
                    for h in range(2):
                        last = nc.tensor.matmul(ps[:, banks + h, :], st[:, s, :], w[:, s0 % RSPL, h * HALF:(h + 1) * HALF],
                                                start=s == 0 and m == 0, stop=s == nk - 1 and m == PASSES - 1)
                last.then_inc(e_used, 1)

            def transpose_x(b):
                pe.wait_ge(xg_in, 16 * (b + 1))
                for k in range(KT):
                    last = nc.tensor.transpose(tiles(4)[:, k, :], xg[:, k * P:(k + 1) * P], ident[:])
                last.then_inc(tx_ok, 1)

            def transpose_h(b):
                pe.wait_ge(hid_ok, b + 1)
                for k in range(DNT):
                    last = nc.tensor.transpose(ps[:, 6, k * P:(k + 1) * P], hid[:, k * P:(k + 1) * P], ident[:])
                last.then_inc(th_ok, 1)

            pe.wait_ge(r_done, 1)
            last_b = nc.tensor.value_load(last_i[0:1, 0:1], min_val=NE - 1, max_val=NBLK - 1)
            transpose_x(0)
            pe.wait_ge(xe_l, 1)
            for s in range(UPT):
                weights(s, s, (xe_hi, xe_lo), s, 0, UPT)
            transpose_x(1)
            with nc.tensor.Fori(1, last_b + 1) as b:
                pe.wait_ge(xe_l, b + 1)
                pe.wait_ge(hid_ok, b)
                for s in range(XT):
                    n = UPT + (b - 1) * XT + s
                    if s == UPT // 2:
                        transpose_h(b - 1)
                    if s == UPT:
                        transpose_x(b + 1)
                        pe.wait_ge(ht_l, b)
                        pe.wait_ge(ye_ok, b)
                    if s < UPT:
                        weights(n, UPT + s, (xe_hi, xe_lo), s, 0, UPT)
                    else:
                        weights(n, UPT + s, (ht_hi, ht_lo), s - UPT, 2, DNT)
            transpose_h(last_b)
            pe.wait_ge(ht_l, last_b + 1)
            pe.wait_ge(ye_ok, last_b + 1)
            for s in range(DNT):
                weights(UPT + last_b * XT + s, UPT + s, (ht_hi, ht_lo), s, 2, DNT)

        @block.scalar
        def _(act):
            act.sem_inc(gate_ok, 1)
            act.sem_inc(o_out, 1)
            act.sem_inc(rt_c, 1)
            act.sem_inc(ye_ok, 1)
            act.sem_inc(ye_out, 16)
            for t in range(TT):
                act.wait_ge(xt_t, t + 1)
                nc.scalar.activation(xt_hi[:, :, t * P:(t + 1) * P], tiles((t % 2) * 2), ACT.Copy).then_inc(xt_h, 1)
            act.wait_ge(wf_in, 32)
            nc.scalar.activation(wf_hi[:], wf_raw[:], ACT.Copy).then_inc(wf_h, 1)
            act.wait_ge(f_mm, 1)
            nc.scalar.activation(fz[:], flat(6)[0:HEADS, :], ACT.Identity, bias=bf[:]).then_inc(f_act, 1)
            act.wait_ge(f_act, 1)
            nc.scalar.activation(fe[:], fz[:], ACT.Abs).then_inc(f_act, 1)
            act.wait_ge(f_act, 2)
            nc.scalar.activation(fc[:], fe[:], ACT.Exp, scale=-1.0).then_inc(f_act, 1)
            act.wait_ge(f_act, 3)
            nc.scalar.activation(fe[:], fc[:], ACT.Ln, bias=1.0).then_inc(f_act, 1)
            act.sem_inc(evac[0], 1)

            def take_out(i, tile):
                kind, b = KINDS[tile], 2 * (tile % 2)
                if kind not in "gcqkv":
                    return
                act.wait_ge(w_used, i * NCH + 2 * tile + 2 + RING)
                if kind == "g":
                    ins = nc.scalar.activation(sg[:], flat(b), ACT.Sigmoid)
                elif kind == "c":
                    ins = nc.scalar.activation(cbuf[:], flat(b), ACT.Copy)
                else:
                    part = "qkv".index(kind)
                    ins = nc.scalar.activation(qkv[:, bass.ds(part * CT + i, 1), :].rearrange("p a n -> p (a n)"), flat(b), ACT.Copy,
                                               scale=DH ** -0.5 if kind == "q" else 1.0)
                ins.then_inc(evac[tile % 2], 1)

            with nc.scalar.Fori(0, CT) as i:
                for c in range(NCH):
                    act.wait_ge(raw_in[c % RING], i * (16 * NCH // RING) + 16 * (c // RING + 1))
                    act.wait_ge(w_used, i * NCH + c + 1)
                    nc.scalar.activation(w_hi[:, c % RING], w_raw[:, c % RING], ACT.Copy).then_inc(hi_ok, 1)
                    if c >= 3 and c % 2 == 1:
                        take_out(i, (c - 3) // 2)
                take_out(i, len(KINDS) - 1)
            act.wait_ge(ln_stats, 2 * TT)
            act.wait_ge(consts, 7)
            nc.scalar.activation(rstd3[:], aggr3[:, :, 1:2].rearrange("p t a -> p (t a)"), ACT.Sqrt, bias=eps[:]).then_inc(std3, 1)
            for t in range(TT):
                act.wait_ge(ln_t2, t + 1)
                for j in range(CT):
                    last = nc.scalar.activation(conv[:, j, t * P:(t + 1) * P], ps[:, bank3(t), j * P:(j + 1) * P], ACT.Silu,
                                                bias=cols[:, ROW_LNB, j:j + 1], scale=cols[:, ROW_LNG, j:j + 1])
                last.then_inc(ln_act, 1)
            with nc.scalar.Fori(0, HEADS // 2) as i:
                def split_qk(u):
                    act.wait_ge(qk_in, 48 * (2 * i + u + 1))
                    if u == 1:
                        act.wait_ge(s_ok, i * 2 * TT + TT)
                    nc.scalar.activation(qk_hi[:], qk_raw[:], ACT.Copy).then_inc(qk_h, 1)

                act.wait_ge(v_t, i + 1)
                nc.scalar.activation(v_hi[:], tiles(4), ACT.Copy).then_inc(v_h, 1)
                split_qk(0)
                for g in range(2 * TT + 3):
                    t = g - 2
                    if t >= 2 and t % 2 == 0:
                        u, r = (t - 2) // TT, (t - 2) % TT
                        act.wait_ge(o_ok, i * TT + t // 2)
                        nc.scalar.activation(qkv[u * DH:(u + 1) * DH, bass.ds(i, 1), r * P:(r + 2) * P].rearrange("p a n -> p (a n)"),
                                             ps[u * DH:(u + 1) * DH, 6, 0:2 * P], ACT.Copy).then_inc(o_out, 1)
                    if 0 <= t < 2 * TT:
                        r = t % TT
                        act.wait_ge(t_ok, i * 2 * TT + t + 1)
                        nc.scalar.activation(pt_hi[:, 0:nkeys(r), (r % 2) * P:(r % 2 + 1) * P], tiles(4)[:, 0:nkeys(r), :],
                                             ACT.Copy).then_inc(pt_h, 1)
                    if g < 2 * TT:
                        r = g % TT
                        act.wait_ge(max_ok, i * 2 * TT + g + 1)
                        nc.scalar.activation(prob[:, g % 2, 0:nkeys(r) * P], flat(2 * (g % 2))[:, 0:nkeys(r) * P], ACT.Exp,
                                             bias=rmax[:, g % 2:g % 2 + 1], accum_out=rsum[:, g % 2:g % 2 + 1]).then_inc(exp_ok, 1)
                    if g == TT - 1:
                        split_qk(1)
            for m in range(NBR):
                if m == 0:
                    act.wait_ge(o_out, HEADS * TT // 2 + 1)
                else:
                    act.wait_ge(used5, m * KT * RING5 + RING5)
                src = (qkv[:, 0:CT, :], conv[:], sc[:])[m]
                nc.scalar.activation(br_hi[:], src, ACT.Copy).then_inc(br_h, 1)
                with nc.scalar.Fori(0, KT) as i:
                    for c in range(RING5):
                        n = (m * KT + i) * RING5 + c
                        act.wait_ge(raw5_in[c], 16 * (m * KT + i + 1))
                        act.wait_ge(used5, n + 1)
                        nc.scalar.activation(w_hi[:, c], w_raw[:, c], ACT.Copy).then_inc(hi5, 1)
                    act.wait_ge(used5, (m * KT + i) * RING5 + 2 + RING5)
                    act.wait_ge(merge_ok, m * KT + i + 1)
                    bias = cols[:].rearrange("p r j -> p (r j)")[:, bass.ds(i + (ROW_BGATE + 2 * m) * CT, 1)]
                    nc.scalar.activation(gate_s[:], flat(0), ACT.Sigmoid, bias=bias).then_inc(gate_ok, 1)

            def split_ms(t):
                nc.scalar.activation(ms_hi[:], merged[:, :, bass.ds(t * P, P)], ACT.Copy).then_inc(ms_h, 1)

            def norm6(t):
                act.wait_ge(ln6, LN_D * t + 3)
                nc.scalar.activation(stat[:, 0, 14:15], stat[:, 0, 13:14], ACT.Sqrt, bias=eps[:]).then_inc(std6, 1)
                act.wait_ge(ln6, LN_D * (t + 1))
                nc.scalar.activation(y1[:], y1[:], ACT.Identity, bias=stat[:, 0, 15:16], scale=stat[:, 0, 14:15]).then_inc(z6, 1)

            def copy_x1t(t):
                act.wait_ge(rt_t1, t + 1)
                nc.scalar.activation(x1t[:], tiles(4), ACT.Copy).then_inc(rt_c, 1)

            for k in range(KT):
                act.wait_ge(wo_in[k % 4], 16 * (k // 4 + 1))
                if k == 0:
                    act.wait_ge(used5, NBR * KT * RING5 + RING5)
                nc.scalar.activation(wo_hi[:, k, :], wo_raw[:, k % 4, :], ACT.Copy).then_inc(wo_h, 1)
            act.wait_ge(merge_ok, NBR * KT + 1)
            split_ms(0)
            act.wait_ge(y_mm, 1)
            split_ms(1)
            norm6(0)
            with nc.scalar.Fori(1, TT - 1) as t:
                act.wait_ge(y_mm, t + 1)
                split_ms(t + 1)
                copy_x1t(t - 1)
                norm6(t)
            copy_x1t(TT - 2)
            norm6(TT - 1)
            copy_x1t(TT - 1)
            act.wait_ge(r_exp, 1)
            nc.scalar.activation(prb[:], rt_t[:], ACT.Exp).then_inc(r_exp, 1)

            def split(n, s0, raw_count):
                act.wait_ge(eraw_in[s0 % RRAW], raw_count)
                act.wait_ge(e_used, n + 1)
                nc.scalar.activation(e_hi[:, s0 % RSPL, :], e_raw[:, s0 % RRAW, :], ACT.Copy).then_inc(e_h, 1)

            def split_x(b):
                act.wait_ge(tx_ok, b + 2)
                nc.scalar.activation(xe_hi[:], tiles(4), ACT.Copy).then_inc(xe_h, 1)

            def silu(b, n_up):
                act.wait_ge(e_used, n_up + RSPL)
                nc.scalar.activation(sil[:], ps[:, 1, :], ACT.Silu).then_inc(sil_ok, 1)

            def split_h(b):
                act.wait_ge(th_ok, b + 1)
                nc.scalar.activation(ht_hi[:], tiles(6, 1), ACT.Copy).then_inc(ht_h, 1)

            def result(b1, extra=0):
                act.wait_ge(e_used, UPT + b1 * XT + RSPL - extra)
                act.wait_ge(ye_out, 16 * b1)
                nc.scalar.activation(ye[:], flat(2), ACT.Copy, scale=slots[:].bitcast(FP32)[:, bass.ds(b1 - 1, 1), 1:2]
                                     .rearrange("p a k -> p (a k)")).then_inc(ye_ok, 1)
                act.wait_ge(ye_ok, b1 + 1)
                act.dma_start(y_d[bass.ds((b1 - 1) * P, P), :], ye[:]).then_inc(ye_out, 16)

            def step(b):
                for s in range(XT):
                    n = UPT + (b - 1) * XT + s
                    split(n, UPT + s, 16 * ((b - 1) + (UPT + s) // RRAW + 1))
                    if s == 3 and not isinstance(b, int):
                        result(b - 1)
                    if s == 7:
                        split_h(b - 1)
                silu(b, UPT + (b - 1) * XT + UPT)
                split_x(b + 1)

            act.wait_ge(r_done, 1)
            last_b = nc.scalar.value_load(last_i[0:1, 0:1], min_val=NE - 1, max_val=NBLK - 1)
            act.wait_ge(fill_out, 16 * CT)
            split_x(0)
            for s in range(UPT):
                split(s, s, 16)
            silu(0, UPT)
            split_x(1)
            step(1)
            with nc.scalar.Fori(2, last_b + 1) as b:
                step(b)
            for s in range(DNT):
                split(UPT + last_b * XT + s, UPT + s, 16 * (last_b + (UPT + s) // RRAW + 1))
            result(last_b)
            split_h(last_b)
            result(last_b + 1, UPT)
            for t in range(TT):
                st = stat[:, t % 2, :]
                act.wait_ge(ln9, LN_D * t + 3)
                nc.scalar.activation(st[:, 14:15], st[:, 13:14], ACT.Sqrt, bias=eps[:]).then_inc(std9, 1)
                act.wait_ge(ln9, LN_D * (t + 1))
                nc.scalar.activation(comb[:, t, :], comb[:, t, :], ACT.Identity, bias=stat[:, t % 2, 15:16],
                                     scale=stat[:, t % 2, 14:15]).then_inc(z9, 1)

        @block.vector
        def _(dve):
            def col(row, j):
                return cols[:].rearrange("p r j -> p (r j)")[:, bass.ds(j + row * CT, 1)]

            class Chain:
                def __init__(self, s, start=0):
                    self.s, self.start, self.n = s, start, 0

                def __call__(self, ins):
                    ins.then_inc(self.s, 1)
                    self.wait()

                def wait(self):
                    self.n += 1
                    dve.wait_ge(self.s, self.start + self.n)

            dve.sem_inc(lo_ok, RING)
            dve.sem_inc(evac[1], 1)
            dve.sem_inc(v_l, 1)
            dve.sem_inc(qk_l, 1)
            dve.sem_inc(pt_l, 1)
            dve.sem_inc(lo5, RING5)
            dve.sem_inc(merge_ok, 1)
            dve.sem_inc(y1_ok, 1)
            dve.sem_inc(lg_ok, 1)
            dve.sem_inc(e_l, RRAW)
            for t in range(TT):
                dve.wait_ge(xt_h, t + 1)
                cut = xt_hi[:, :, t * P:(t + 1) * P]
                nc.vector.tensor_tensor(xt_lo[:, :, t * P:(t + 1) * P], tiles((t % 2) * 2), cut, ALU.subtract).then_inc(xt_l, 1)
            dve.wait_ge(wf_h, 1)
            nc.vector.tensor_tensor(wf_lo[:], wf_raw[:], wf_hi[:], ALU.subtract).then_inc(wf_l, 1)
            dve.wait_ge(cols_t, 1)
            nc.vector.tensor_copy(cols[:], ps[:, 4, 0:CT * ROWS].rearrange("p (j r) -> p r j", j=CT)).then_inc(cols_ok, 1)
            link = Chain(f_dve)
            dve.wait_ge(f_act, 4)
            link(nc.vector.scalar_tensor_tensor(fz[:], fz[:], 0.0, fe[:], ALU.min, ALU.subtract))
            link(nc.vector.memset(fe[:], 1.0))
            link(nc.vector.tensor_tensor_scan(fc[:], fe[:], fz[:], 0.0, ALU.mult, ALU.add))
            link(nc.vector.tensor_scalar(fz[:], fc[:], -1.0, None, ALU.mult))
            dve.wait_ge(cols_ok, 1)
            dve.wait_ge(pads, 2)

            def take_out(i, tile, link):
                kind, b = KINDS[tile], 2 * (tile % 2)
                if kind not in "ahb":
                    return
                dve.wait_ge(w_used, i * NCH + 2 * tile + 2 + RING)
                if kind == "a":
                    dve.wait_ge(evac[0], i * 4 + 2)
                    nc.vector.tensor_tensor(upad[:, CTAPS - 1:], flat(b), sg[:], ALU.mult).then_inc(evac[tile % 2], 1)
                    dve.wait_ge(evac[1], i * 4 + 2)
                elif kind == "h":
                    dve.wait_ge(evac[0], i * 4 + 3)
                    nc.vector.tensor_tensor(hpad[:, STAPS - 1:], flat(b), cbuf[:], ALU.mult).then_inc(evac[tile % 2], 1)
                    dve.wait_ge(evac[1], i * 4 + 3)
                    link(nc.vector.tensor_scalar(scacc[:], hpad[:, 0:SEQ], col(ROW_SCW, i), None, ALU.mult))
                    for j in range(1, STAPS):
                        link(nc.vector.scalar_tensor_tensor(scacc[:], hpad[:, j:j + SEQ], col(ROW_SCW + j, i), scacc[:], ALU.mult, ALU.add))
                else:
                    dst = sc[:, bass.ds(i, 1), :].rearrange("p a n -> p (a n)")
                    nc.vector.tensor_tensor(dst, flat(b), scacc[:], ALU.mult).then_inc(evac[tile % 2], 1)

            with nc.vector.Fori(0, CT) as i:
                link = Chain(conv_chain, i * CONV_LINKS)
                dst = conv[:, bass.ds(i, 1), :].rearrange("p a n -> p (a n)")
                taps = list(range(CTAPS))
                for c in range(NCH):
                    dve.wait_ge(hi_ok, i * NCH + c + 1)
                    nc.vector.tensor_tensor(w_lo[:, c % RING], w_raw[:, c % RING], w_hi[:, c % RING], ALU.subtract).then_inc(lo_ok, 1)
                    if c >= 3 and c % 2 == 1:
                        take_out(i, (c - 3) // 2, link)
                    if c >= 5:
                        for j in taps[:3]:
                            if j == 0:
                                link(nc.vector.tensor_scalar(dst, upad[:, 0:SEQ], col(ROW_CONVW, i), col(ROW_CONVB, i), ALU.mult, ALU.add))
                            else:
                                link(nc.vector.scalar_tensor_tensor(dst, upad[:, j:j + SEQ], col(ROW_CONVW + j, i), dst, ALU.mult, ALU.add))
                        taps = taps[3:]
                assert not taps and link.n == CONV_LINKS
            link = Chain(ln_dve)
            for t in range(TT):
                dve.wait_ge(ln_t, t + 1)
                nc.vector.bn_stats(stat3[:, t, 0:6], ps[:, bank3(t), :]).then_inc(ln_stats, 1)
            dve.wait_ge(ln_stats, TT)
            for t in range(TT):
                nc.vector.bn_aggr(aggr3[:, t, :], stat3[:, t, 0:6]).then_inc(ln_stats, 1)
            dve.wait_ge(std3, 1)
            link(nc.vector.reciprocal(rstd3[:], rstd3[:]))
            for t in range(TT):
                if t >= 2:
                    dve.wait_ge(ln_t2, t - 1)
                nc.vector.tensor_scalar(yln[:, t % 2, :], ps[:, bank3(t), :], aggr3[:, t, 0:1], rstd3[:, t:t + 1],
                                        ALU.subtract, ALU.mult).then_inc(ln_dve, 1)
            with nc.vector.Fori(0, HEADS // 2) as i:
                def split_qk(u):
                    dve.wait_ge(qk_h, 2 * i + u + 1)
                    nc.vector.tensor_tensor(qk_lo[:], qk_raw[:], qk_hi[:], ALU.subtract).then_inc(qk_l, 1)

                dve.wait_ge(v_h, i + 1)
                nc.vector.tensor_tensor(v_lo[:], tiles(4), v_hi[:], ALU.subtract).then_inc(v_l, 1)
                split_qk(0)
                for g in range(2 * TT + 2):
                    t = g - 2
                    if g < 2 * TT:
                        r = g % TT
                        dve.wait_ge(s_ok, i * 2 * TT + g + 1)
                        nc.vector.tensor_reduce(rmax[:, g % 2:g % 2 + 1], flat(2 * (g % 2))[:, 0:nkeys(r) * P], AX.X, ALU.max,
                                                negate=True).then_inc(max_ok, 1)
                    if t >= 0:
                        r = t % TT
                        dve.wait_ge(pt_h, i * 2 * TT + t + 1)
                        cut = (slice(None), slice(0, nkeys(r)), slice((r % 2) * P, (r % 2 + 1) * P))
                        nc.vector.tensor_tensor(pt_lo[cut], tiles(4)[:, 0:nkeys(r), :], pt_hi[cut], ALU.subtract).then_inc(pt_l, 1)
                    if g < 2 * TT:
                        dve.wait_ge(exp_ok, i * 2 * TT + g + 1)
                        nc.vector.reciprocal(rinv[:, g % 2:g % 2 + 1], rsum[:, g % 2:g % 2 + 1]).then_inc(inv_ok, 1)
                    if g == TT - 1:
                        split_qk(1)
            for m in range(NBR):
                dve.wait_ge(br_h, m + 1)
                src = (qkv[:, 0:CT, :], conv[:], sc[:])[m]
                nc.vector.tensor_tensor(br_lo[:], src, br_hi[:], ALU.subtract).then_inc(br_l, 1)

                def split5(i, c):
                    dve.wait_ge(hi5, (m * KT + i) * RING5 + c + 1)
                    nc.vector.tensor_tensor(w_lo[:, c], w_raw[:, c], w_hi[:, c], ALU.subtract).then_inc(lo5, 1)

                def merge(i):
                    dve.wait_ge(used5, (m * KT + i + 1) * RING5 + RING5)
                    dve.wait_ge(gate_ok, m * KT + i + 2)
                    dst = merged[:, bass.ds(i, 1), :].rearrange("p a n -> p (a n)")
                    if m == 0:
                        nc.vector.tensor_tensor(dst, flat(2), gate_s[:], ALU.mult).then_inc(merge_ok, 1)
                    else:
                        nc.vector.tensor_tensor(gate_s[:], flat(2), gate_s[:], ALU.mult).then_inc(merge_chain, 1)
                        dve.wait_ge(merge_chain, (m - 1) * KT + i + 1)
                        nc.vector.tensor_tensor(dst, dst, gate_s[:], ALU.add).then_inc(merge_ok, 1)

                for c in range(RING5):
                    split5(0, c)
                with nc.vector.Fori(1, KT) as i:
                    split5(i, 0)
                    split5(i, 1)
                    merge(i - 1)
                    split5(i, 2)
                merge(KT - 1)

            def split_ms(t):
                dve.wait_ge(ms_h, t + 1)
                nc.vector.tensor_tensor(ms_lo[:], merged[:, :, bass.ds(t * P, P)], ms_hi[:], ALU.subtract).then_inc(ms_l, 1)

            def statistics(src, st, link, std, count):
                link(nc.vector.bn_stats(st[:, 0:6], src[:, 0:HALF]))
                nc.vector.bn_stats(st[:, 6:12], src[:, HALF:D]).then_inc(link.s, 1)
                link.wait()
                dve.sem_inc(passed_dve, 1)
                link(nc.vector.bn_aggr(st[:, 12:14], st[:, 0:12]))
                dve.wait_ge(std, count)
                link(nc.vector.reciprocal(st[:, 14:15], st[:, 14:15]))
                link(nc.vector.tensor_scalar(st[:, 15:16], st[:, 12:13], st[:, 14:15], -1.0, ALU.mult, ALU.mult))

            def residual(t):
                dve.wait_ge(y_mm, t + 1)
                dve.wait_ge(xres_in, 16 * (t + 1))
                nc.vector.scalar_tensor_tensor(y1[:], x_res[:], ALPHA, flat(0), ALU.mult, ALU.add).then_inc(y1_ok, 1)
                dve.wait_ge(y1_ok, t + 2)

            def norm6(t, x1_used):
                link = Chain(ln6, LN_D * t)
                statistics(y1, stat[:, 0, :], link, std6, t + 1)
                assert link.n == LN_D
                dve.wait_ge(z6, t + 1)
                nc.vector.tensor_tensor(y1[:], y1[:], lng1[:], ALU.mult).then_inc(g6, 1)
                dve.wait_ge(g6, t + 1)
                if x1_used:
                    dve.wait_ge(rt_t1, t)
                    dve.wait_ge(x1_out, 16 * t)
                nc.vector.tensor_tensor(x1[:], y1[:], lnb1[:], ALU.add).then_inc(x1_ok, 1)

            def take_logits(t):
                dve.wait_ge(rt_mm, t + 1)
                nc.vector.tensor_tensor(logits[:, bass.ds(t, 1), :].rearrange("p a n -> p (a n)"), ps[:, 6, 0:NE],
                                        b_rt[:], ALU.add).then_inc(lg_ok, 1)

            for k in range(KT):
                dve.wait_ge(wo_h, k + 1)
                nc.vector.tensor_tensor(wo_lo[:, k, :], wo_raw[:, k % 4, :], wo_hi[:, k, :], ALU.subtract).then_inc(wo_l, 1)
            split_ms(0)
            dve.wait_ge(par6_in, 64)
            residual(0)
            split_ms(1)
            norm6(0, False)
            with nc.vector.Fori(1, TT - 1) as t:
                residual(t)
                split_ms(t + 1)
                norm6(t, True)
                take_logits(t - 1)
            residual(TT - 1)
            norm6(TT - 1, True)
            take_logits(TT - 2)
            take_logits(TT - 1)

            link = Chain(r_chain)
            dve.wait_ge(lg_ok, TT + 1)
            dve.wait_ge(r_const, 10)

            def wide(v, n):
                return v.unsqueeze(len(v.shape)).to_broadcast(list(v.shape) + [n])

            def groups(v):
                return v[:].rearrange("p t (g e) -> p t g e", e=EPG)

            V = nc.vector
            tmax, tsum, trec, v1, v2, vs, vr = (byt[:, j, :] for j in range(7))
            m1, m2, first, score, ohg, gsc = (grp[:, j] for j in range(6))
            link(V.tensor_reduce(tmax, logits[:], AX.X, ALU.max))
            link(V.tensor_tensor(rt_t[:], logits[:], wide(tmax, NE), ALU.subtract))
            dve.sem_inc(r_exp, 1)
            dve.wait_ge(r_exp, 2)
            link(V.tensor_reduce(tsum, prb[:], AX.X, ALU.add))
            link(V.reciprocal(trec, tsum))
            link(V.tensor_tensor(prb[:], prb[:], wide(trec, NE), ALU.mult))
            link(V.tensor_reduce(m1, groups(prb), AX.X, ALU.max))
            link(V.tensor_tensor(groups(rt_t), groups(prb), wide(m1, EPG), ALU.is_equal))
            link(V.tensor_tensor(groups(rt_t), groups(rt_t), kneg[:], ALU.mult))
            link(V.tensor_reduce(first, groups(rt_t), AX.X, ALU.max))
            link(V.tensor_tensor(groups(oh1), groups(rt_t), wide(first, EPG), ALU.is_equal))
            link(V.scalar_tensor_tensor(p2[:], oh1[:], -2.0, prb[:], ALU.mult, ALU.add))
            link(V.tensor_reduce(m2, groups(p2), AX.X, ALU.max))
            link(V.tensor_tensor(groups(rt_t), groups(p2), wide(m2, EPG), ALU.is_equal))
            link(V.tensor_tensor(groups(rt_t), groups(rt_t), kneg[:], ALU.mult))
            link(V.tensor_reduce(first, groups(rt_t), AX.X, ALU.max))
            link(V.tensor_tensor(groups(oh2), groups(rt_t), wide(first, EPG), ALU.is_equal))
            link(V.tensor_tensor(score, m1, m2, ALU.add))
            link(V.tensor_reduce(tmax, score, AX.X, ALU.max))
            link(V.tensor_tensor(gsc, score, wide(tmax, NG), ALU.is_equal))
            link(V.tensor_tensor(gsc, gsc, gneg[:], ALU.mult))
            link(V.tensor_reduce(tmax, gsc, AX.X, ALU.max))
            link(V.tensor_tensor(ohg, gsc, wide(tmax, NG), ALU.is_equal))
            link(V.tensor_tensor(groups(oh1), groups(oh1), wide(ohg, EPG), ALU.mult))
            link(V.tensor_tensor(groups(oh2), groups(oh2), wide(ohg, EPG), ALU.mult))
            link(V.tensor_tensor(sel_b[:], oh1[:], oh2[:], ALU.add))
            dve.sem_inc(r_sel, 1)
            link(V.tensor_tensor(m1, m1, ohg, ALU.mult))
            link(V.tensor_reduce(v1, m1, AX.X, ALU.add))
            link(V.tensor_tensor(m2, m2, ohg, ALU.mult))
            link(V.tensor_reduce(v2, m2, AX.X, ALU.add))
            link(V.tensor_tensor(vs, v1, v2, ALU.add))
            link(V.reciprocal(vr, vs))
            gate_bits = pairs[:].bitcast(FP32)
            for k, v in enumerate((v1, v2)):
                link(V.tensor_tensor(gate_bits[:, k, :, 1:2].rearrange("p t a -> p (t a)"), v, vr, ALU.mult))
            dve.wait_ge(r_cnt, 1)
            before, per_tile = (ps[:, b, 0:TT * NE].rearrange("p (t e) -> p t e", e=NE) for b in (0, 1))
            link(V.memset(tcum[:, 0, :], 0.0))
            for t in range(1, TT):
                link(V.tensor_tensor(tcum[:, t, :], tcum[:, t - 1, :], per_tile[:, t - 1, :], ALU.add))
            count, extra, upto, diff, start, inc32, lowb, eb = (ev[:, j, :] for j in range(8))
            link(V.tensor_tensor(count, tcum[:, TT - 1, :], per_tile[:, TT - 1, :], ALU.add))
            link(V.tensor_tensor(gt[:], wide(count, TT - 1), thr[:], ALU.is_gt))
            link(V.tensor_reduce(extra, gt[:], AX.X, ALU.add))
            link(V.tensor_tensor_scan(upto, ones_e[:], extra, 0.0, ALU.mult, ALU.add))
            link(V.tensor_scalar(last_i[:], upto[:, NE - 1:NE], float(NE - 1), None, ALU.add))
            link(V.tensor_tensor(start, upto, extra, ALU.subtract))
            link(V.tensor_scalar(start, start, float(NE - 1), None, ALU.add))
            link(V.tensor_tensor(diff, start, biota[:, 0:NE], ALU.subtract))
            link(V.tensor_scalar(diff, diff, float(P), None, ALU.mult))
            link(V.tensor_scalar(start, biota[:, 0:NE], float(P), None, ALU.mult))
            link(V.tensor_tensor(dest[:], before, tcum[:], ALU.add))

            def by_tile(v):
                return v.unsqueeze(1).to_broadcast([P, TT, NE])

            link(V.scalar_tensor_tensor(rt_t[:], dest[:], float(P), by_tile(diff), ALU.is_ge, ALU.mult))
            link(V.tensor_tensor(dest[:], dest[:], by_tile(start), ALU.add))
            link(V.tensor_tensor(dest[:], dest[:], rt_t[:], ALU.add))
            for k, oh in enumerate((oh1, oh2)):
                link(V.tensor_tensor(rt_u[:], dest[:], oh[:], ALU.mult))
                link(V.tensor_reduce(byt[:, 7, :], rt_u[:], AX.X, ALU.add))
                link(V.tensor_copy(dest_i[:, k, :], byt[:, 7, :]))
            link(V.tensor_scalar(inc32, upto, float(NE), None, ALU.add))
            link(V.tensor_tensor(bmap[:], wide(biota[:], NE), inc32.unsqueeze(1).to_broadcast([P, NBLK, NE]), ALU.is_ge))
            link(V.tensor_reduce(rt_u[:].rearrange("p t e -> p (t e)")[:, 0:NBLK], bmap[:], AX.X, ALU.add))
            link(V.scalar_tensor_tensor(rt_t[:].rearrange("p t e -> p (t e)")[:, 0:NBLK], biota[:], float(NE), biota[:], ALU.is_lt, ALU.mult))
            link(V.tensor_tensor(rt_u[:].rearrange("p t e -> p (t e)")[:, 0:NBLK], rt_u[:].rearrange("p t e -> p (t e)")[:, 0:NBLK],
                                 rt_t[:].rearrange("p t e -> p (t e)")[:, 0:NBLK], ALU.add))
            link(V.tensor_scalar(expert_i[:], rt_u[:].rearrange("p t e -> p (t e)")[:, 0:NBLK], float(NE - 1), None, ALU.min))
            dve.sem_inc(r_done, 1)

            def split(n, s0):
                dve.wait_ge(e_h, n + 1)
                nc.vector.tensor_tensor(e_lo[:, s0 % RSPL, :], e_raw[:, s0 % RRAW, :], e_hi[:, s0 % RSPL, :], ALU.subtract).then_inc(e_l, 1)

            def split_x(b):
                dve.wait_ge(xe_h, b + 1)
                nc.vector.tensor_tensor(xe_lo[:], tiles(4), xe_hi[:], ALU.subtract).then_inc(xe_l, 1)

            def hidden(b):
                dve.wait_ge(sil_ok, b + 1)
                nc.vector.tensor_tensor(hid[:], ps[:, 0, :], sil[:], ALU.mult).then_inc(hid_ok, 1)

            def split_h(b):
                dve.wait_ge(ht_h, b + 1)
                nc.vector.tensor_tensor(ht_lo[:], tiles(6, 1), ht_hi[:], ALU.subtract).then_inc(ht_l, 1)

            last_b = nc.vector.value_load(last_i[0:1, 0:1], min_val=NE - 1, max_val=NBLK - 1)
            split_x(0)
            for s in range(UPT):
                split(s, s)
            hidden(0)
            split_x(1)
            with nc.vector.Fori(1, last_b + 1) as b:
                for s in range(XT):
                    split(UPT + (b - 1) * XT + s, UPT + s)
                    if s == 7:
                        split_h(b - 1)
                hidden(b)
                split_x(b + 1)
            for s in range(DNT):
                split(UPT + last_b * XT + s, UPT + s)
            split_h(last_b)
            dve.wait_ge(par9_in, 32)
            for t in range(TT + 1):
                if t < TT:
                    dve.wait_ge(add2[t], 16)
                    link = Chain(ln9, LN_D * t)
                    statistics(comb[:, t, :], stat[:, t % 2, :], link, std9, t + 1)
                if t >= 1:
                    u = t - 1
                    dve.wait_ge(z9, u + 1)
                    nc.vector.tensor_tensor(comb[:, u, :], comb[:, u, :], lng2[:], ALU.mult).then_inc(g9, 1)
                    dve.wait_ge(g9, u + 1)
                    if u >= 2:
                        dve.wait_ge(out_dma[u % 2], 16 * (u // 2))
                    nc.vector.tensor_tensor(zout[:, u % 2, :], comb[:, u, :], lnb2[:], ALU.add).then_inc(out_ok, 1)


_INS = ["x", "w_in", "b_forget", "conv_w", "conv_b", "conv_ln_g", "conv_ln_b", "sc_w", "w_branch", "w_gate",
        "b_gate", "w_out", "ln1_g", "ln1_b", "w_up", "w_down", "ln2_g", "ln2_b", "w_router", "b_router"]


def kernel(**inputs):
    import concourse.bacc as bacc
    from concourse.bass_utils import run_bass_kernel_spmd

    nc = bacc.Bacc("TRN2", target_bir_lowering=False, num_devices=1)
    arrays = {"in_" + n: np.ascontiguousarray(inputs[n]) for n in _INS}
    args = [nc.dram_tensor(n, a.shape, mybir.dt.from_np(a.dtype), kind="ExternalInput").ap() for n, a in arrays.items()]
    out = nc.dram_tensor("out_0", (1, SEQ, D), FP32, kind="ExternalOutput").ap()
    program(nc, *args, out)
    return run_bass_kernel_spmd(nc, [arrays], core_ids=[0]).results[0]["out_0"]
```

```python
import numpy as np
import concourse.bass as bass
from concourse import mybir
from contextlib import ExitStack

FP32 = mybir.dt.float32
FP32R = mybir.dt.float32r
BF16 = mybir.dt.bfloat16
I32 = mybir.dt.int32
ALU = mybir.AluOpType
ACT = mybir.ActivationFunctionType
AX = mybir.AxisListType

P = 128
SEQ = 1024
D = 1024
KT = D // P
TT = SEQ // P
HALF = 512
HEADS, DH = 8, 64
W = 512
CT = W // P
CTAPS, STAPS = 31, 3
NBR = 3
Q0, K0, V0, F0 = 0, W, 2 * W, 3 * W
A0 = F0 + HEADS
G0, B0, C0, H0 = A0 + W, A0 + 2 * W, A0 + 3 * W, A0 + 4 * W
KC = 4
RING = 4
RING5 = 3
ROW_CONVW = 0
ROW_SCW = CTAPS
ROW_CONVB = ROW_SCW + STAPS
ROW_LNG = ROW_CONVB + 1
ROW_LNB = ROW_LNG + 1
ROW_BGATE = ROW_LNB + 1
ROWS = ROW_BGATE + NBR * D // W
NE, NG, EPG, TOPK = 32, 8, 4, 2
FF = 512
NBLK = NE + (SEQ * TOPK) // P
NB1 = NBLK + 1
NO_TOK, NO_ROW = 4 * SEQ, 8 * SEQ
UPT, DNT = D // P, FF // P
XT = UPT + DNT
RRAW, RSPL = 12, 6
ALPHA = 2.0 ** 0.25
EPS = 1e-5
MASKED = -1e30
KB = 1024
PASSES = 3
CONV_LINKS = CTAPS + STAPS
LN_D = 5

KINDS = ("g", "a", "c", "h", "b", "q", "k", "v")
COL = dict(g=G0, a=A0, c=C0, h=H0, b=B0, q=Q0, k=K0, v=V0)
NCH = 2 * len(KINDS)
RAW2 = 16 * CT * NCH // RING


def program(nc, x, w_in, b_forget, conv_w, conv_b, conv_ln_g, conv_ln_b, sc_w,
            w_branch, w_gate, b_gate, w_out, ln1_g, ln1_b, w_up, w_down,
            ln2_g, ln2_b, w_router, b_router, out):
    ctx = ExitStack()
    base = (nc.sbuf_base + 127) // 128 * 128

    def at(name, shape, dtype, kb):
        return nc.alloc_sbuf_tensor_at(name, shape, dtype, offset=base + int(kb * KB))

    def sem(name):
        return ctx.enter_context(nc.semaphore(name))

    with ctx:
        ctx.enter_context(nc.sbuf_tensor("whole_map", [P, 207 * KB // 4], FP32))
        xt_hi = at("xt_hi", [P, KT, SEQ], FP32R, 0)
        xt_lo = at("xt_lo", [P, KT, SEQ], FP32R, 32)
        x_raw = at("x_raw", [P, TT, D], FP32, 64)
        qkv = at("qkv", [P, 3 * CT, SEQ], FP32, 64)
        conv = at("conv", [P, CT, SEQ], FP32, 112)
        sc1 = at("sc1", [P, SEQ], FP32, 128)
        w_raw = at("w_raw", [P, RING, KC, P], FP32, 144)
        w_hi = at("w_hi", [P, RING, KC, P], FP32R, 152)
        w_lo = at("w_lo", [P, RING, KC, P], FP32R, 160)
        upad = at("upad", [P, CTAPS - 1 + SEQ], FP32, 168)
        sg = at("sg", [P, SEQ], FP32, 173)
        hpad = at("hpad", [P, STAPS - 1 + SEQ], FP32, 177)
        cbuf = at("cbuf", [P, SEQ], FP32, 182)
        scacc = at("scacc", [P, SEQ], FP32, 182)
        fz = at("fz", [HEADS, SEQ], FP32, 187)
        fe = at("fe", [HEADS, SEQ], FP32, 191)
        fc = at("fc", [HEADS, SEQ], FP32, 195)
        rows = at("rows", [ROWS, W], FP32, 199)
        wf_raw = at("wf_raw", [P, KT, HEADS], FP32, 201)
        wf_hi = at("wf_hi", [P, KT, HEADS], FP32R, 201.5)
        wf_lo = at("wf_lo", [P, KT, HEADS], FP32R, 202)
        yln = at("yln", [P, 2, W], FP32, 168)
        stat3 = at("stat3", [P, TT, 8], FP32, 172)
        aggr3 = at("aggr3", [P, TT, 2], FP32, 172.5)
        rstd3 = at("rstd3", [P, TT], FP32, 172.75)
        ident = at("ident", [P, P], FP32, 204)
        ident_b = at("ident_b", [P, P], BF16, 204.5)
        mask_b = at("mask_b", [P, 2 * P], BF16, 204.75)
        cols = at("cols", [P, ROWS, CT], FP32, 205.25)
        bf = at("bf", [HEADS, 1], FP32, 206)
        stat = at("stat", [P, 2, 16], FP32, 206.125)
        eps = at("eps", [P, 1], FP32, 206.0625)
        rmax = at("rmax", [P, 2], FP32, 206.25)
        rsum = at("rsum", [P, 2], FP32, 206.3125)
        rinv = at("rinv", [P, 2], FP32, 206.375)
        AUG = DH + 2
        v_hi = at("v_hi", [P, TT, P], FP32R, 112)
        v_lo = at("v_lo", [P, TT, P], FP32R, 116)
        prob = at("prob", [P, 2, SEQ], FP32, 120)
        qk_raw = at("qk_raw", [AUG, 2, SEQ], FP32, 128)
        vt_raw = at("vt_raw", [P, SEQ], FP32, 136)
        qk_hi = at("qk_hi", [AUG, 2, 2, SEQ], FP32R, 140)
        qk_lo = at("qk_lo", [AUG, 2, 2, SEQ], FP32R, 156)
        pt_hi = at("pt_hi", [P, 2, TT, 2 * P], FP32R, 172)
        pt_lo = at("pt_lo", [P, 2, TT, 2 * P], FP32R, 188)
        br_raw = at("br_raw", [P, CT, SEQ], FP32, 112)
        merged = at("merged", [P, KT, SEQ], FP32, 80)
        br_hi = at("br_hi", [P, CT, SEQ], FP32R, 168)
        br_lo = at("br_lo", [P, CT, SEQ], FP32R, 184)
        gate_s = at("gate_s", [P, SEQ], FP32, 200)
        wo_raw = at("wo_raw", [P, 4, D], FP32, 64)
        wo_hi = at("wo_hi", [P, KT, D], FP32R, 0)
        wo_lo = at("wo_lo", [P, KT, D], FP32R, 32)
        ms_hi = at("ms_hi", [P, KT, P], FP32R, 112)
        ms_lo = at("ms_lo", [P, KT, P], FP32R, 116)
        x_res = at("x_res", [P, D], FP32, 120)
        y1 = at("y1", [P, D], FP32, 124)
        x1 = at("x1", [P, D], FP32, 128)
        x1t = at("x1t", [P, KT, P], FP32, 132)
        lg_t = at("lg_t", [NE, P], FP32, 70)
        lng1 = at("lng1", [P, D], FP32, 136)
        lnb1 = at("lnb1", [P, D], FP32, 140)
        w_rt = at("w_rt", [P, KT, NE], FP32, 64)
        b_rt = at("b_rt", [P, NE], FP32, 65)
        logits = at("logits", [P, TT, NE], FP32, 65.125)
        kneg = at("kneg", [P, TT, NG, EPG], FP32, 66.125)
        gneg = at("gneg", [P, TT, NG], FP32, 67.125)
        thr = at("thr", [P, NE, TT - 1], FP32, 67.375)
        tri_b = at("tri_b", [P, P], BF16, 68.25)
        one_b = at("one_b", [P, P], BF16, 68.5)
        biota = at("biota", [P, NB1], FP32, 68.75)
        ones_e = at("ones_e", [P, NE], FP32, 69)
        tokm = at("tokm", [P, TT], FP32, 69.125)
        rowm = at("rowm", [P, TOPK, TT], FP32, 69.25)
        iota_p = at("iota_p", [P, P], FP32, 69.5)
        prb = at("prb", [P, TT, NE], FP32, 112)
        p2 = at("p2", [P, TT, NE], FP32, 113)
        oh1 = at("oh1", [P, TT, NE], FP32, 114)
        oh2 = at("oh2", [P, TT, NE], FP32, 115)
        rt_t = at("rt_t", [P, TT, NE], FP32, 116)
        rt_u = at("rt_u", [P, TT, NE], FP32, 117)
        sel_b = at("sel_b", [P, TT, NE], BF16, 118)
        dest = at("dest", [P, TT, NE], FP32, 119)
        tcum = at("tcum", [P, TT, NE], FP32, 120)
        gt = at("gt", [P, NE, TT - 1], FP32, 121)
        grp = at("grp", [P, 8, TT, NG], FP32, 122)
        ev = at("ev", [P, 8, NE], FP32, 124)
        byt = at("byt", [P, 8, TT], FP32, 125)
        dest_f = at("dest_f", [P, TOPK, TT], FP32, 125.25)
        gates = at("gates", [P, TOPK, TT], FP32, 125.5)
        dest_i = at("dest_i", [P, TOPK, TT], I32, 125.75)
        blk_i = at("blk_i", [P, TOPK, TT], I32, 126)
        blk_f = at("blk_f", [P, TOPK, TT], FP32, 126.25)
        rank_f = at("rank_f", [P, TOPK, TT], FP32, 126.5)
        bmap = at("bmap", [P, NBLK, NE], FP32, 127)
        by_rank = at("by_rank", [P, TOPK, TT, P], FP32, 48)
        by_blk = at("by_blk", [P, TOPK, TT, NB1], FP32, 56)
        vals = at("vals", [P, TOPK, TT, 3, NB1], FP32, 133)
        expert_i = at("expert_i", [P, NBLK], I32, 203)
        last_i = at("last_i", [P, 1], I32, 203.1875)
        tail_i = at("tail_i", [P, 1], I32, 203.9375)
        tok_tab = at("tok_tab", [P, NB1], I32, 203.21875)
        row_tab = at("row_tab", [P, NB1], I32, 203.4375)
        gate_tab = at("gate_tab", [P, NB1], FP32, 203.65625)
        tok_i = at("tok_i", [P, 1], I32, 203.875)
        row_i = at("row_i", [P, 1], I32, 203.90625)
        e_hi = at("e_hi", [P, RSPL, D], FP32R, 0)
        e_lo = at("e_lo", [P, RSPL, D], FP32R, 24)
        xg = at("xg", [P, D], FP32, 48)
        xe_hi = at("xe_hi", [P, KT, P], FP32R, 52)
        xe_lo = at("xe_lo", [P, KT, P], FP32R, 56)
        ht_hi = at("ht_hi", [P, DNT, P], FP32R, 60)
        ht_lo = at("ht_lo", [P, DNT, P], FP32R, 62)
        ye = at("ye", [P, D], FP32, 76)
        e_first = at("e_first", [P, UPT, D], FP32, 80)
        sil = at("sil", [P, FF], FP32, 112)
        hid = at("hid", [P, FF], FP32, 114)
        e_raw = at("e_raw", [P, RRAW, D], FP32, 144)
        comb = at("comb", [P, TT, D], FP32, 80)
        zout = at("zout", [P, 2, D], FP32, 116)
        lng2 = at("lng2", [P, D], FP32, 124)
        lnb2 = at("lnb2", [P, D], FP32, 128)

        ps = ctx.enter_context(nc.psum_tensor("ps", [P, 8, HALF], FP32))

        forget_d = nc.dram_tensor("forget_d", [HEADS, 2, 2, SEQ], FP32, kind="Internal").ap()
        conv_d = nc.dram_tensor("conv_d", [W, SEQ], FP32, kind="Internal").ap()
        sc_d = nc.dram_tensor("sc_d", [W, SEQ], FP32, kind="Internal").ap()
        x1_d = nc.dram_tensor("x1_d", [SEQ, D], FP32, kind="Internal").ap()
        y_d = nc.dram_tensor("y_d", [TOPK * SEQ, D], FP32, kind="Internal").ap()

        rows_in, wf_in, forget_out = sem("rows_in"), sem("wf_in"), sem("forget_out")
        consts, pads, xt_t, xt_h, xt_l = sem("consts"), sem("pads"), sem("xt_t"), sem("xt_h"), sem("xt_l")
        cols_t, cols_ok, wf_h, wf_l, f_mm, f_act, f_dve = (sem(n) for n in (
            "cols_t", "cols_ok", "wf_h", "wf_l", "f_mm", "f_act", "f_dve"))
        raw_in = [sem(f"raw_in{i}") for i in range(RING)]
        hi_ok = sem("hi_ok")
        lo_ok = sem("lo_ok")
        w_used = sem("w_used")
        evac = [sem("evac0"), sem("evac1")]
        conv_chain = sem("conv_chain")
        ln_stats = sem("ln_stats")
        ln_t, ln_dve, ln_t2, ln_act = sem("ln_t"), sem("ln_dve"), sem("ln_t2"), sem("ln_act")
        sc_out, conv_out, br_in = sem("sc_out"), sem("conv_out"), sem("br_in")
        qk_in, v_in = sem("qk_in"), sem("v_in")
        qk_h, qk_l = sem("qk_h"), sem("qk_l")
        v_t, v_h, v_l = sem("v_t"), sem("v_h"), sem("v_l")
        s_ok, max_ok, exp_ok, inv_ok, norm_ok = sem("s_ok"), sem("max_ok"), sem("exp_ok"), sem("inv_ok"), sem("norm_ok")
        t_ok, pt_h, pt_l, o_ok, o_out = sem("t_ok"), sem("pt_h"), sem("pt_l"), sem("o_ok"), sem("o_out")
        hi5, lo5, used5 = sem("hi5"), sem("lo5"), sem("used5")
        br_h, br_l, gate_ok, merge_ok, merge_chain = sem("br_h"), sem("br_l"), sem("gate_ok"), sem("merge_ok"), sem("merge_chain")
        wo_in = [sem(f"wo_in{i}") for i in range(4)]
        wo_h, wo_l, par6_in, xres_in = sem("wo_h"), sem("wo_l"), sem("par6_in"), sem("xres_in")
        ms_h, ms_l, y_mm, y1_ok, ln6, x1_ok, x1_out = (sem(n) for n in (
            "ms_h", "ms_l", "y_mm", "y1_ok", "ln6", "x1_ok", "x1_out"))
        rt_t1, rt_c, rt_m, rt_lc, rt_mm, lg_ok = (sem(n) for n in ("rt_t1", "rt_c", "rt_m", "rt_lc", "rt_mm", "lg_ok"))
        r_const, r_chain, r_exp, r_sel, r_cnt, r_vals, r_tab, r_done = (sem(n) for n in (
            "r_const", "r_chain", "r_exp", "r_sel", "r_cnt", "r_vals", "r_tab", "r_done"))
        eraw_in = [sem(f"eraw_in{i}") for i in range(RRAW)]
        e_h, e_used = sem("e_h"), sem("e_used")
        e_all = sem("e_all")
        e_l = sem("e_l")
        first_in = [sem(f"first_in{s}") for s in range(UPT)]
        xg_zero, tok_ok, row_ok, xg_in = sem("xg_zero"), sem("tok_ok"), sem("row_ok"), sem("xg_in")
        tx_ok, xe_h, xe_l, sil_ok, hid_ok = sem("tx_ok"), sem("xe_h"), sem("xe_l"), sem("sil_ok"), sem("hid_ok")
        th_ok, ht_h, ht_l, ye_ok, ye_out = sem("th_ok"), sem("ht_h"), sem("ht_l"), sem("ye_ok"), sem("ye_out")
        par9_in, comb_in, comb_s = sem("par9_in"), sem("comb_in"), sem("comb_s")
        add1 = [sem(f"add1_{t}") for t in range(4)]
        add2 = [sem(f"add2_{t}") for t in range(TT)]
        ln9, out_ok, out_dma = sem("ln9"), sem("out_ok"), [sem("out_dma0"), sem("out_dma1")]

        std3, std6, std9 = sem("std3"), sem("std6"), sem("std9")

        passed_sp, passed_pool, passed_dve, passed_pe = (sem(n) for n in ("passed_sp", "passed_pool", "passed_dve", "passed_pe"))

        block = ctx.enter_context(nc.Block())

        def flat(b, n=2):
            return ps[:, b:b + n, :].rearrange("p a b -> p (a b)")

        def tiles(b, n=2):
            return ps[:, b:b + n, :].rearrange("p a (k n) -> p (a k) n", n=P)

        def bank3(t):
            return (4, 5, 0, 1, 2, 3, 6, 7)[t]

        def nkeys(r):
            return 2 * (r // 2) + 2

        @block.sync
        def _(sp):
            for t in range(TT):
                sp.dma_start(x_raw[:, t, :], x[0, t * P:(t + 1) * P, :]).then_inc(first_in[t], 16)
            for lo, hi, src in ((ROW_CONVW, ROW_SCW, conv_w[0]), (ROW_SCW, ROW_CONVB, sc_w[0]), (ROW_CONVB, ROW_LNG, conv_b),
                                (ROW_LNG, ROW_LNB, conv_ln_g), (ROW_LNB, ROW_BGATE, conv_ln_b),
                                (ROW_BGATE, ROWS, b_gate[0].rearrange("n (h w) -> (n h) w", w=W))):
                sp.dma_start(rows[lo:hi, :], src).then_inc(rows_in, 16)
            sp.dma_start(wf_raw[:], w_in[0, :, F0:A0].rearrange("(k p) n -> p k n", p=P),
                         allow_slow_non_contiguous=True).then_inc(wf_in, 16)
            sp.dma_start(bf[:], b_forget.rearrange("a h -> h a"), allow_slow_non_contiguous=True).then_inc(wf_in, 16)
            with nc.sync.Fori(0, CT) as i:
                for c in range(NCH):
                    kind, half = KINDS[c // 2], c % 2
                    src = w_in[0, half * KC * P:(half + 1) * KC * P, bass.ds(i * P + COL[kind], P)]
                    sp.wait_ge(lo_ok, i * NCH + c + 1)
                    sp.sem_inc(passed_sp, 1)
                    sp.dma_start(w_raw[:, c % RING], src.rearrange("(k p) n -> p k n", p=P)).then_inc(raw_in[c % RING], 16)
                sp.wait_ge(evac[0], i * (len(KINDS) // 2) + 4)
                sp.dma_start(sc_d[bass.ds(i * P, P), :], sc1[:]).then_inc(sc_out, 16)
            for t in range(TT):
                sp.wait_ge(ln_act, t + 1)
                sp.dma_start(conv_d[:, t * P:(t + 1) * P].rearrange("(j p) n -> p j n", p=P), conv[:, :, t * P:(t + 1) * P]).then_inc(conv_out, 16)
            sp.wait_ge(sc_out, 16 * CT + 16)
            sp.wait_ge(evac[1], 1 + CT * len(KINDS) // 2)
            sp.wait_ge(forget_out, 64)
            def load_pair(i):
                if not isinstance(i, int):
                    sp.wait_ge(v_t, 2 * i)
                sp.dma_start(vt_raw[:], qkv[:, bass.ds(2 * CT + i, 1), :].rearrange("p a n -> p (a n)")).then_inc(v_in, 16)
                for u in range(2):
                    sp.wait_ge(qk_l, 2 * i + u + 1)
                    for s in range(2):
                        sp.dma_start(qk_raw[0:DH, s, :], qkv[u * DH:(u + 1) * DH, bass.ds(s * CT + i, 1), :].rearrange("p a n -> p (a n)")).then_inc(qk_in, 16)
                    sp.dma_start(qk_raw[DH:AUG, :, :], forget_d[bass.ds(2 * i + u, 1)].rearrange("a s r n -> (a r) s n")).then_inc(qk_in, 16)

            load_pair(0)
            with nc.sync.Fori(1, HEADS // 2) as i:
                load_pair(i)
            sp.wait_ge(o_out, HEADS * TT // 2 + 1)
            for n in range(NBR):
                with nc.sync.Fori(0, KT) as i:
                    for c in range(RING5):
                        sp.wait_ge(lo5, (n * KT + i) * RING5 + c + 1)
                        if c < 2:
                            src = w_gate[0, n, c * KC * P:(c + 1) * KC * P, bass.ds(i * P, P)]
                        else:
                            src = w_branch[0, n, :, bass.ds(i * P, P)]
                        sp.dma_start(w_raw[:, c], src.rearrange("(k p) n -> p k n", p=P)).then_inc(raw_in[c], 16)
                if n < NBR - 1:
                    sp.wait_ge(br_l, (n + 1) * CT)
                    src = (conv_d, sc_d)[n]
                    sp.dma_start(br_raw[:], src.rearrange("(j p) n -> p j n", p=P)).then_inc(br_in, 16)
                if n == 0:
                    sp.wait_ge(br_l, CT)
                    for k in range(4):
                        sp.dma_start(wo_raw[:, k, :], w_out[0, k * P:(k + 1) * P, :]).then_inc(wo_in[k], 16)
            for k in range(4, KT):
                sp.wait_ge(wo_l, k - 3)
                sp.dma_start(wo_raw[:, k % 4, :], w_out[0, k * P:(k + 1) * P, :]).then_inc(wo_in[k % 4], 16)
            sp.wait_ge(merge_ok, NBR * KT + 1)
            sp.wait_ge(wo_l, KT)
            sp.dma_start(w_rt[:], w_router.rearrange("(k p) n -> p k n", p=P)).then_inc(par6_in, 16)
            sp.dma_start(b_rt[:], b_router.partition_broadcast(P)).then_inc(par6_in, 16)
            sp.dma_start(lng1[:], ln1_g[0].partition_broadcast(P)).then_inc(par6_in, 16)
            sp.dma_start(lnb1[:], ln1_b[0].partition_broadcast(P)).then_inc(par6_in, 16)

            def load(n, s0, src):
                sp.wait_ge(e_l, n + 1)
                sp.dma_start(e_raw[:, s0, :], src).then_inc(eraw_in[s0], 16)

            sp.dma_start(x_res[:], x[0, 0:P, :]).then_inc(xres_in, 16)
            for s in range(XT):
                load(s, s, w_up[0, 1, s * P:(s + 1) * P, :] if s < UPT else w_down[0, 0, (s - UPT) * P:(s - UPT + 1) * P, :])
            sp.wait_ge(x1_ok, 1)
            sp.dma_start(x1_d[0:P, :], x1[:]).then_inc(x1_out, 16)
            with nc.sync.Fori(1, TT) as t:
                sp.wait_ge(y1_ok, t + 1)
                sp.dma_start(x_res[:], x[0, bass.ds(t * P, P), :]).then_inc(xres_in, 16)
                sp.wait_ge(x1_ok, t + 1)
                sp.dma_start(x1_d[bass.ds(t * P, P), :], x1[:]).then_inc(x1_out, 16)
            sp.wait_ge(ms_l, 2 * TT)
            for s in range(UPT):
                sp.dma_start(e_first[:, s, :], w_up[0, 0, s * P:(s + 1) * P, :]).then_inc(first_in[s], 16)
            sp.wait_ge(r_done, 1)
            last_b = nc.sync.value_load(last_i[0:1, 0:1], min_val=NE - 1, max_val=NBLK - 1)

            def load_step(b, n0):
                up_e = nc.sync.value_load(expert_i[0:1, bass.ds(b, 1)], min_val=0, max_val=NE - 1)
                dn_e = nc.sync.value_load(expert_i[0:1, bass.ds(b - 1, 1)], min_val=0, max_val=NE - 1)
                for s in range(XT):
                    if s < UPT:
                        src = w_up[0, bass.ds(up_e, 1), s * P:(s + 1) * P, :]
                    else:
                        src = w_down[0, bass.ds(dn_e, 1), (s - UPT) * P:(s - UPT + 1) * P, :]
                    load(n0 + s, s, src.rearrange("a p n -> (a p) n"))

            load_step(2, XT)
            sp.dma_start(lng2[:], ln2_g[0].partition_broadcast(P)).then_inc(par9_in, 16)
            sp.dma_start(lnb2[:], ln2_b[0].partition_broadcast(P)).then_inc(par9_in, 16)
            sp.wait_ge(x1_out, 16 * TT)
            sp.dma_start(comb[:], x1_d.rearrange("(t p) n -> p t n", p=P)).then_inc(comb_in, 16)
            with nc.sync.Fori(3, last_b + 1) as b:
                load_step(b, (b - 1) * XT)
            last_e = nc.sync.value_load(expert_i[0:1, bass.ds(last_b, 1)], min_val=0, max_val=NE - 1)
            for s in range(DNT):
                src = w_down[0, bass.ds(last_e, 1), s * P:(s + 1) * P, :]
                load(last_b * XT + s, s, src.rearrange("a p n -> (a p) n"))
            for t in range(TT):
                sp.wait_ge(out_ok, t + 1)
                sp.dma_start(out[0, t * P:(t + 1) * P, :], zout[:, t % 2, :]).then_inc(out_dma[t % 2], 16)
            for u in range(2):
                sp.wait_ge(out_dma[u], 16 * TT // 2)

        @block.gpsimd
        def _(pool):
            pool.sem_inc(qk_l, 1)
            nc.gpsimd.memset(ident[:], 0.0).then_inc(consts, 1)
            nc.gpsimd.memset(mask_b[:, 0:P], 0.0).then_inc(consts, 1)
            nc.gpsimd.memset(mask_b[:, P:2 * P], MASKED).then_inc(consts, 1)
            pool.wait_ge(consts, 3)
            nc.gpsimd.affine_select(out=ident[:], in_=ident[:], compare_op=ALU.not_equal, fill=1.0,
                                    base=0, pattern=[[-1, P]], channel_multiplier=1).then_inc(consts, 1)
            nc.gpsimd.affine_select(out=mask_b[:, 0:P], in_=mask_b[:, 0:P], compare_op=ALU.is_ge, fill=MASKED,
                                    base=0, pattern=[[-1, P]], channel_multiplier=1).then_inc(consts, 1)
            pool.wait_ge(consts, 5)
            nc.gpsimd.tensor_copy(ident_b[:], ident[:]).then_inc(consts, 1)
            nc.gpsimd.memset(eps[:], EPS).then_inc(consts, 1)
            nc.gpsimd.memset(upad[:, 0:CTAPS - 1], 0.0).then_inc(pads, 1)
            nc.gpsimd.memset(hpad[:, 0:STAPS - 1], 0.0).then_inc(pads, 1)
            pool.wait_ge(f_dve, 4)
            for side, row, src in ((0, 0, fc), (0, 1, fe), (1, 0, fe), (1, 1, fz)):
                pool.dma_start(forget_d[:, side, row, :], src[:]).then_inc(forget_out, 16)
            with nc.gpsimd.Fori(0, HEADS // 2) as i:
                for u in range(2):
                    pool.wait_ge(qk_h, 2 * i + u + 1)
                    nc.gpsimd.tensor_tensor(qk_lo[:, u], qk_raw[:], qk_hi[:, u], ALU.subtract).then_inc(qk_l, 1)
            pool.wait_ge(merge_ok, NBR * KT + 1)
            pool.wait_ge(wo_l, KT)

            def steps(dst, pattern, base, channel_multiplier):
                nc.gpsimd.iota(dst, pattern, base=base, channel_multiplier=channel_multiplier,
                               allow_small_or_imprecise_dtypes=True).then_inc(r_const, 1)

            steps(kneg[:], [[0, TT], [0, NG], [-1, EPG]], EPG, 0)
            steps(gneg[:], [[0, TT], [-1, NG]], NG, 0)
            steps(thr[:], [[0, NE], [P, TT - 1]], P, 0)
            steps(biota[:], [[1, NB1]], 0, 0)
            steps(iota_p[:], [[1, P]], 0, 0)
            steps(tokm[:], [[P, TT]], -NO_TOK, 1)
            steps(rowm[:], [[SEQ, TOPK], [P, TT]], -NO_ROW, 1)
            nc.gpsimd.memset(one_b[:], 1.0).then_inc(r_const, 1)
            nc.gpsimd.memset(ones_e[:], 1.0).then_inc(r_const, 1)
            pool.wait_ge(r_const, 9)
            nc.gpsimd.affine_select(out=tri_b[:], in_=one_b[:], compare_op=ALU.is_ge, fill=0.0,
                                    base=-1, pattern=[[1, P]], channel_multiplier=-1).then_inc(r_const, 1)

            def gather(b):
                if not isinstance(b, int) or b > 0:
                    pool.wait_ge(xg_in, 16 * b)
                    pool.sem_inc(passed_pool, 1)
                nc.gpsimd.tensor_copy(tok_i[:], tok_tab[:, bass.ds(b, 1)]).then_inc(tok_ok, 1)
                pool.wait_ge(tok_ok, b + 1)
                pool.wait_ge(tx_ok, b + 1)
                pool.sem_inc(passed_pool, 1)
                nc.gpsimd.indirect_dma_start(out=xg[:], out_offset=None, in_=x1_d,
                                             in_offset=bass.IndirectOffsetOnAxis(ap=tok_i[:], axis=0),
                                             bounds_check=SEQ - 1, oob_is_err=False).then_inc(xg_in, 16)

            def scatter(b1):
                if not isinstance(b1, int):
                    pool.wait_ge(ye_out, 16 * (b1 - 1))
                    pool.sem_inc(passed_pool, 1)
                nc.gpsimd.tensor_copy(row_i[:], row_tab[:, bass.ds(b1 - 1, 1)]).then_inc(row_ok, 1)
                pool.wait_ge(row_ok, b1)
                pool.wait_ge(ye_ok, b1 + 1)
                pool.sem_inc(passed_pool, 1)
                nc.gpsimd.indirect_dma_start(out=y_d, out_offset=bass.IndirectOffsetOnAxis(ap=row_i[:], axis=0),
                                             in_=ye[:], in_offset=None,
                                             bounds_check=TOPK * SEQ - 1, oob_is_err=False).then_inc(ye_out, 16)

            pool.wait_ge(r_vals, 1)
            pool.wait_ge(y_mm, TT)
            pool.wait_ge(r_tab, 1)
            nc.gpsimd.memset(xg[:], 0.0).then_inc(xg_zero, 1)
            pool.wait_ge(x1_out, 16 * TT)
            pool.wait_ge(xg_zero, 1)
            pool.wait_ge(r_done, 1)
            tail = nc.gpsimd.value_load(tail_i[0:1, 0:1], min_val=NE - 3, max_val=NBLK - 3)
            for b in range(3):
                gather(b)
            pool.wait_ge(comb_in, 16)
            nc.gpsimd.tensor_scalar(comb[:], comb[:], ALPHA, None, ALU.mult).then_inc(comb_s, 1)
            gather(3)
            scatter(1)
            gather(4)
            with nc.gpsimd.Fori(5, tail + 4) as b:
                scatter(b - 3)
                gather(b)
            for k in range(3):
                scatter(tail + 1 + k)
            pool.wait_ge(ye_out, 16 * (tail + 3))
            pool.wait_ge(comb_s, 1)
            pool.sem_inc(passed_pool, 1)

            def add(k, t, done):
                row = k * SEQ + t * P
                pool.dma_start(comb[:, t, :], y_d[row:row + P, :], accum_op=ALU.add).then_inc(done, 16)

            for t in range(TT + 1):
                if t < TT:
                    add(0, t, add1[t % 4])
                if t >= 1:
                    pool.wait_ge(add1[(t - 1) % 4], 16 * ((t - 1) // 4 + 1))
                    add(1, t - 1, add2[t - 1])

        @block.tensor
        def _(pe):
            def product(o, terms, nk, cut, start, stop):
                for k in nk:
                    for n, (st, mv) in enumerate(terms):
                        for h, c0, c1 in cut:
                            last = nc.tensor.matmul(o(h, c1 - c0), st(k), mv(k, c0, c1),
                                                    start=start and k == nk[0] and n == 0,
                                                    stop=h in stop and k == nk[-1] and n == PASSES - 1)
                return last

            HALVES = ((0, 0, HALF), (1, HALF, 2 * HALF))
            pe.sem_inc(w_used, RING)
            pe.sem_inc(used5, RING5)
            pe.sem_inc(e_used, RSPL)
            pe.sem_inc(tx_ok, 1)
            pe.wait_ge(consts, 6)
            for t in range(TT):
                if t >= 2:
                    pe.wait_ge(xt_l, t - 1)
                pe.wait_ge(first_in[t], 16)
                for k in range(KT):
                    last = nc.tensor.transpose(tiles((t % 2) * 2)[:, k, :], x_raw[:, t, k * P:(k + 1) * P], ident[:])
                last.then_inc(xt_t, 1)
            pe.wait_ge(rows_in, 16 * 6)
            for j in range(CT):
                last = nc.tensor.transpose(ps[:, 4, j * ROWS:(j + 1) * ROWS], rows[:, j * P:(j + 1) * P], ident[0:ROWS, 0:ROWS])
            last.then_inc(cols_t, 1)
            pe.wait_ge(xt_l, TT)
            pe.wait_ge(wf_l, 1)
            product(lambda h, n: ps[0:HEADS, 6 + h, :],
                    [(lambda k, w=w: w[:, k, :], lambda k, a, b, v=v: v[:, k, a:b]) for w, v in ((wf_hi, xt_hi), (wf_hi, xt_lo), (wf_lo, xt_hi))],
                    range(KT), HALVES, True, (0, 1)).then_inc(f_mm, 1)
            with nc.tensor.Fori(0, CT) as i:
                for c in range(NCH):
                    tile, half = c // 2, c % 2
                    if half == 0:
                        pe.wait_ge(evac[tile % 2], i * (len(KINDS) // 2) + tile // 2 + 1)
                    pe.wait_ge(lo_ok, i * NCH + c + 1 + RING)
                    product(lambda h, n: ps[:, 2 * (tile % 2) + h, :],
                            [(lambda k, w=w: w[:, c % RING, k - half * KC, :], lambda k, a, b, v=v: v[:, k, a:b])
                             for w, v in ((w_hi, xt_hi), (w_hi, xt_lo), (w_lo, xt_hi))],
                            range(half * KC, (half + 1) * KC), HALVES, half == 0, (0, 1) if half else ()).then_inc(w_used, 1)
            pe.wait_ge(conv_chain, CT * CONV_LINKS)
            for t in range(TT):
                if t == 6:
                    pe.wait_ge(f_act, 1)
                if t == 2:
                    pe.wait_ge(evac[0], 1 + CT * len(KINDS) // 2)
                    pe.wait_ge(evac[1], 1 + CT * len(KINDS) // 2)
                for j in range(CT):
                    last = nc.tensor.transpose(ps[:, bank3(t), j * P:(j + 1) * P], conv[:, j, t * P:(t + 1) * P], ident[:])
                last.then_inc(ln_t, 1)
            for t in range(TT):
                pe.wait_ge(ln_dve, t + 2)
                for j in range(CT):
                    last = nc.tensor.transpose(ps[:, bank3(t), j * P:(j + 1) * P], yln[:, t % 2, j * P:(j + 1) * P], ident[:])
                last.then_inc(ln_t2, 1)
            def scores(i, g):
                u, r, n = g // TT, g % TT, i * 2 * TT + g
                nk = nkeys(r) * P
                if r == 0:
                    pe.wait_ge(qk_l, 2 * i + u + 2)
                if not isinstance(n, int) or n >= 2:
                    pe.wait_ge(exp_ok, n - 1)
                b = 2 * (g % 2)
                m0 = r * P
                cut = [(h, a, min(a + HALF, nk)) for h, a in enumerate(range(0, nk, HALF))]
                product(lambda h, n: ps[:, b + h, 0:n],
                        [(lambda k, q=q: q[:, u, 0, r * P:(r + 1) * P], lambda k, a, e, v=v: v[:, u, 1, a:e])
                         for q, v in ((qk_hi, qk_hi), (qk_hi, qk_lo), (qk_lo, qk_hi))],
                        [0], cut, True, [h for h, _, _ in cut if h != m0 // HALF])
                nc.tensor.matmul(flat(b)[:, m0:nk], ident_b[:], mask_b[:, 0:nk - m0],
                                 start=False, stop=True).then_inc(s_ok, 1)

            def transpose_p(i, t):
                n = i * 2 * TT + t
                pe.wait_ge(norm_ok, n + 1)
                pe.wait_ge(pt_l, n + 1)
                for k in range(nkeys(t % TT)):
                    last = nc.tensor.transpose(tiles(4)[:, k, :], prob[:, t % 2, k * P:(k + 1) * P], ident[:])
                last.then_inc(t_ok, 1)

            def attend(i, t):
                pe.wait_ge(pt_l, i * 2 * TT + t + 2)
                pe.wait_ge(o_out, i * TT + (t + 1) // 2)
                if t < 6:
                    pe.wait_ge(v_l, 2 * i + 2 + (t > 3))
                nk = nkeys(t % TT)
                for k in range(nk):
                    for n, (v, p) in enumerate(((v_hi, pt_hi), (v_hi, pt_lo), (v_lo, pt_hi))):
                        last = nc.tensor.matmul(ps[:, 6, 0:2 * P], v[:, k, :], p[:, t // 2 % 2, k, :],
                                                start=k == 0 and n == 0, stop=k == nk - 1 and n == PASSES - 1)
                last.then_inc(o_ok, 1)

            def transpose_v(i, half):
                if half == 0:
                    pe.wait_ge(v_in, 16 * (i + 1))
                pe.wait_ge(v_l, 2 * i + half + 1)
                for k in range(KC):
                    kk = half * KC + k
                    last = nc.tensor.transpose(ps[:, 7, k * P:(k + 1) * P], vt_raw[:, kk * P:(kk + 1) * P], ident[:])
                last.then_inc(v_t, 1)

            def pe_step(i, g):
                scores(i, g)
                for lag, what in ((2, transpose_p), (3, attend)):
                    j, t = (i, g - lag) if g >= lag else (i - 1, g - lag + 2 * TT)
                    if (what is transpose_p or t % 2) and not (isinstance(j, int) and j < 0):
                        what(j, t)
                if g in (2, 3):
                    transpose_v(i, g - 2)

            for g in range(2 * TT):
                pe_step(0, g)
            with nc.tensor.Fori(1, HEADS // 2) as i:
                for g in range(2 * TT):
                    pe_step(i, g)
            last_pair = HEADS // 2 - 1
            attend(last_pair, 2 * TT - 3)
            transpose_p(last_pair, 2 * TT - 2)
            transpose_p(last_pair, 2 * TT - 1)
            attend(last_pair, 2 * TT - 1)
            for m in range(NBR):
                with nc.tensor.Fori(0, KT) as i:
                    for c in range(RING5):
                        pe.wait_ge(lo5, (m * KT + i) * RING5 + c + 1 + RING5)
                        if c == 0:
                            pe.wait_ge(gate_ok, m * KT + i + 1)
                        if c == 2:
                            pe.wait_ge(br_l, (m + 1) * CT)
                            pe.wait_ge(merge_ok, m * KT + i + 1)
                        mh, ml = (xt_hi, xt_lo) if c < 2 else (br_hi, br_lo)
                        k0 = KC * c if c < 2 else 0
                        product(lambda h, n: ps[:, (0 if c < 2 else 2) + h, :],
                                [(lambda k, w=w: w[:, c, k - k0, :], lambda k, a, b, v=v: v[:, k, a:b])
                                 for w, v in ((w_hi, mh), (w_hi, ml), (w_lo, mh))],
                                range(k0, k0 + KC), HALVES, c != 1, (0, 1) if c else ()).then_inc(used5, 1)

            def project(t, k0, k1):
                if k0 == 0:
                    pe.wait_ge(y1_ok, t + 1)
                for k in range(k0, k1):
                    if k % KC == 0:
                        pe.wait_ge(ms_l, 2 * t + k // KC + 1)
                    if isinstance(t, int) and t == 0:
                        pe.wait_ge(wo_l, k + 1)
                    last = product(lambda h, n: ps[:, h, :],
                                   [(lambda k, s=s: s[:, k, :], lambda k, a, b, v=v: v[:, k, a:b]) for s, v in ((ms_hi, wo_hi), (ms_hi, wo_lo), (ms_lo, wo_hi))],
                                   [k], HALVES, k == 0, (0, 1) if k == KT - 1 else ())
                if k1 == KT:
                    last.then_inc(y_mm, 1)

            def route_x(t):
                pe.wait_ge(x1_ok, t + 1)
                pe.wait_ge(rt_c, t + 1)
                for k in range(KT):
                    last = nc.tensor.transpose(tiles(4)[:, k, :], x1[:, k * P:(k + 1) * P], ident[:])
                last.then_inc(rt_t1, 1)

            def route_mm(t):
                pe.wait_ge(rt_c, t + 2)
                for k in range(KT):
                    last = nc.tensor.matmul(ps[0:NE, 7, 0:P], w_rt[:, k, :], x1t[:, k, :], start=k == 0, stop=k == KT - 1)
                last.then_inc(rt_m, 1)

            def route_t(t):
                pe.wait_ge(rt_lc, t + 1)
                pe.wait_ge(lg_ok, t + 1)
                pe.sem_inc(passed_pe, 1)
                nc.tensor.transpose(ps[:, 6, 0:NE], lg_t[:], ident[0:NE, 0:NE]).then_inc(rt_mm, 1)

            SPLIT = 6
            project(0, 0, KT)
            pe.wait_ge(par6_in, 64)
            project(1, 0, SPLIT)
            route_x(0)
            project(1, SPLIT, KT)
            route_mm(0)
            with nc.tensor.Fori(2, TT) as t:
                project(t, 0, SPLIT)
                route_t(t - 2)
                route_x(t - 1)
                project(t, SPLIT, KT)
                route_mm(t - 1)
            route_t(TT - 2)
            route_x(TT - 1)
            route_mm(TT - 1)
            route_t(TT - 1)
            pe.wait_ge(r_sel, 1)
            pe.wait_ge(r_const, 10)
            selv = sel_b[:].rearrange("p t e -> p (t e)")
            nc.tensor.matmul(ps[:, 0, 0:TT * NE], tri_b[:], selv, start=True, stop=True)
            nc.tensor.matmul(ps[:, 1, 0:TT * NE], one_b[:], selv, start=True, stop=True).then_inc(r_cnt, 1)
            pe.wait_ge(r_vals, 1)
            for k in range(TOPK):
                for t in range(TT):
                    last = nc.tensor.matmul(ps[:, 7, 0:3 * NB1], by_rank[:, k, t, :], vals[:, k, t].rearrange("p c b -> p (c b)"),
                                            start=k == 0 and t == 0, stop=k == TOPK - 1 and t == TT - 1)
            last.then_inc(r_tab, 1)

            def weights(n, s0, stat, s, banks, nk):
                pe.wait_ge(e_all, n + 1)
                sh, sl = stat
                for m, (st, w) in enumerate(((sh, e_hi), (sh, e_lo), (sl, e_hi))):
                    for h in range(2):
                        last = nc.tensor.matmul(ps[:, banks + h, :], st[:, s, :], w[:, s0 % RSPL, h * HALF:(h + 1) * HALF],
                                                start=s == 0 and m == 0, stop=s == nk - 1 and m == PASSES - 1)
                last.then_inc(e_used, 1)

            def transpose_x(b):
                pe.wait_ge(xg_in, 16 * (b + 1))
                for k in range(KT):
                    last = nc.tensor.transpose(tiles(4)[:, k, :], xg[:, k * P:(k + 1) * P], ident[:])
                last.then_inc(tx_ok, 1)

            def transpose_h(b):
                pe.wait_ge(hid_ok, b + 1)
                for k in range(DNT):
                    last = nc.tensor.transpose(ps[:, 6, k * P:(k + 1) * P], hid[:, k * P:(k + 1) * P], ident[:])
                last.then_inc(th_ok, 1)

            pe.wait_ge(r_done, 1)
            last_b = nc.tensor.value_load(last_i[0:1, 0:1], min_val=NE - 1, max_val=NBLK - 1)
            transpose_x(0)
            pe.wait_ge(xe_l, 1)
            for s in range(UPT):
                weights(s, s, (xe_hi, xe_lo), s, 0, UPT)
            transpose_x(1)
            with nc.tensor.Fori(1, last_b + 1) as b:
                pe.wait_ge(xe_l, b + 1)
                pe.wait_ge(hid_ok, b)
                for s in range(XT):
                    n = UPT + (b - 1) * XT + s
                    if s == UPT // 2:
                        transpose_h(b - 1)
                    if s == UPT:
                        transpose_x(b + 1)
                        pe.wait_ge(ht_l, b)
                        pe.wait_ge(ye_ok, b)
                    if s < UPT:
                        weights(n, UPT + s, (xe_hi, xe_lo), s, 0, UPT)
                    else:
                        weights(n, UPT + s, (ht_hi, ht_lo), s - UPT, 2, DNT)
            transpose_h(last_b)
            pe.wait_ge(ht_l, last_b + 1)
            pe.wait_ge(ye_ok, last_b + 1)
            for s in range(DNT):
                weights(UPT + last_b * XT + s, UPT + s, (ht_hi, ht_lo), s, 2, DNT)

        @block.scalar
        def _(act):
            act.sem_inc(gate_ok, 1)
            act.sem_inc(o_out, 1)
            act.sem_inc(rt_c, 1)
            act.sem_inc(ye_ok, 1)
            for t in range(TT):
                act.wait_ge(xt_t, t + 1)
                nc.scalar.activation(xt_hi[:, :, t * P:(t + 1) * P], tiles((t % 2) * 2), ACT.Copy).then_inc(xt_h, 1)
            act.wait_ge(wf_in, 32)
            nc.scalar.activation(wf_hi[:], wf_raw[:], ACT.Copy).then_inc(wf_h, 1)
            act.sem_inc(evac[0], 1)

            def take_out(i, tile):
                kind, b = KINDS[tile], 2 * (tile % 2)
                if kind not in "gcqkv":
                    return
                act.wait_ge(w_used, i * NCH + 2 * tile + 2 + RING)
                if kind == "g":
                    ins = nc.scalar.activation(sg[:], flat(b), ACT.Sigmoid)
                elif kind == "c":
                    ins = nc.scalar.activation(cbuf[:], flat(b), ACT.Copy)
                else:
                    part = "qkv".index(kind)
                    ins = nc.scalar.activation(qkv[:, bass.ds(part * CT + i, 1), :].rearrange("p a n -> p (a n)"), flat(b), ACT.Copy,
                                               scale=DH ** -0.5 if kind == "q" else 1.0)
                ins.then_inc(evac[tile % 2], 1)

            with nc.scalar.Fori(0, CT) as i:
                for c in range(NCH):
                    act.wait_ge(raw_in[c % RING], i * (16 * NCH // RING) + 16 * (c // RING + 1))
                    act.wait_ge(w_used, i * NCH + c + 1)
                    nc.scalar.activation(w_hi[:, c % RING], w_raw[:, c % RING], ACT.Copy).then_inc(hi_ok, 1)
                    if c >= 3 and c % 2 == 1:
                        take_out(i, (c - 3) // 2)
                take_out(i, len(KINDS) - 1)
            act.wait_ge(f_mm, 1)
            nc.scalar.activation(fz[:], flat(6)[0:HEADS, :], ACT.Identity, bias=bf[:]).then_inc(f_act, 1)
            act.wait_ge(f_act, 1)
            nc.scalar.activation(fe[:], fz[:], ACT.Abs).then_inc(f_act, 1)
            act.wait_ge(f_act, 2)
            nc.scalar.activation(fc[:], fe[:], ACT.Exp, scale=-1.0).then_inc(f_act, 1)
            act.wait_ge(f_act, 3)
            nc.scalar.activation(fe[:], fc[:], ACT.Ln, bias=1.0).then_inc(f_act, 1)
            act.wait_ge(ln_stats, 2 * TT)
            act.wait_ge(consts, 7)
            nc.scalar.activation(rstd3[:], aggr3[:, :, 1:2].rearrange("p t a -> p (t a)"), ACT.Sqrt, bias=eps[:]).then_inc(std3, 1)
            for t in range(TT):
                act.wait_ge(ln_t2, t + 1)
                for j in range(CT):
                    last = nc.scalar.activation(conv[:, j, t * P:(t + 1) * P], ps[:, bank3(t), j * P:(j + 1) * P], ACT.Silu,
                                                bias=cols[:, ROW_LNB, j:j + 1], scale=cols[:, ROW_LNG, j:j + 1])
                last.then_inc(ln_act, 1)
            def split_qk(head, u):
                act.wait_ge(qk_in, 48 * (head + 1))
                nc.scalar.activation(qk_hi[:, u], qk_raw[:], ACT.Copy).then_inc(qk_h, 1)

            def exponential(i, g):
                n, cut = i * 2 * TT + g, nkeys(g % TT) * P
                act.wait_ge(max_ok, n + 1)
                nc.scalar.activation(prob[:, g % 2, 0:cut], flat(2 * (g % 2))[:, 0:cut], ACT.Exp,
                                     bias=rmax[:, g % 2:g % 2 + 1], accum_out=rsum[:, g % 2:g % 2 + 1]).then_inc(exp_ok, 1)

            def split_pt(i, t):
                r = t % TT
                act.wait_ge(t_ok, i * 2 * TT + t + 1)
                nc.scalar.activation(pt_hi[:, t // 2 % 2, 0:nkeys(r), (r % 2) * P:(r % 2 + 1) * P], tiles(4)[:, 0:nkeys(r), :],
                                     ACT.Copy).then_inc(pt_h, 1)

            def output(i, t):
                u, r = t // TT, t % TT - 1
                act.wait_ge(o_ok, i * TT + (t + 1) // 2)
                nc.scalar.activation(qkv[u * DH:(u + 1) * DH, bass.ds(i, 1), r * P:(r + 2) * P].rearrange("p a n -> p (a n)"),
                                     ps[u * DH:(u + 1) * DH, 6, 0:2 * P], ACT.Copy).then_inc(o_out, 1)

            def split_v(i, half):
                act.wait_ge(v_t, 2 * i + half + 1)
                nc.scalar.activation(v_hi[:, half * KC:(half + 1) * KC, :], tiles(7, 1), ACT.Copy).then_inc(v_h, 1)

            def act_step(i, g, last_pair=False):
                for lag, what in ((4, output), (2, split_pt), (0, exponential)):
                    j, t = (i, g - lag) if g >= lag else (i - 1, g - lag + 2 * TT)
                    if (what is not output or t % 2) and not (isinstance(j, int) and j < 0):
                        what(j, t)
                if g in (2, 3):
                    split_v(i, g - 2)
                if g == 4:
                    split_qk(2 * i + 1, 1)
                if g == 12 and not last_pair:
                    split_qk(2 * i + 2, 0)

            act.wait_ge(conv_out, 16 * TT)
            split_qk(0, 0)
            for g in range(2 * TT):
                act_step(0, g)
            with nc.scalar.Fori(1, HEADS // 2 - 1) as i:
                for g in range(2 * TT):
                    act_step(i, g)
            for g in range(2 * TT):
                act_step(HEADS // 2 - 1, g, True)
            split_pt(HEADS // 2 - 1, 2 * TT - 2)
            output(HEADS // 2 - 1, 2 * TT - 3)
            split_pt(HEADS // 2 - 1, 2 * TT - 1)
            output(HEADS // 2 - 1, 2 * TT - 1)
            for m in range(NBR):
                def chunk(i, c):
                    act.wait_ge(raw_in[c], RAW2 + 16 * (m * KT + i + 1))
                    act.wait_ge(used5, (m * KT + i) * RING5 + c + 1)
                    nc.scalar.activation(w_hi[:, c], w_raw[:, c], ACT.Copy).then_inc(hi5, 1)

                def gate(i):
                    act.wait_ge(used5, (m * KT + i) * RING5 + 2 + RING5)
                    act.wait_ge(merge_ok, m * KT + i + 1)
                    bias = cols[:].rearrange("p r j -> p (r j)")[:, bass.ds(i + (ROW_BGATE + 2 * m) * CT, 1)]
                    nc.scalar.activation(gate_s[:], flat(0), ACT.Sigmoid, bias=bias).then_inc(gate_ok, 1)

                chunk(0, 0)
                chunk(0, 1)
                if m == 0:
                    act.wait_ge(o_out, HEADS * TT // 2 + 1)
                else:
                    act.wait_ge(used5, m * KT * RING5 + RING5)
                    act.wait_ge(br_in, 16 * m)
                src = (qkv[:, 0:CT, :], br_raw[:], br_raw[:])[m]
                for k in range(CT):
                    nc.scalar.activation(br_hi[:, k], src[:, k], ACT.Copy).then_inc(br_h, 1)
                chunk(0, 2)
                gate(0)
                with nc.scalar.Fori(1, KT) as i:
                    for c in range(RING5):
                        chunk(i, c)
                    gate(i)

            def split_ms(t):
                nc.scalar.activation(ms_hi[:], merged[:, :, bass.ds(t * P, P)], ACT.Copy).then_inc(ms_h, 1)

            def norm6(t):
                act.wait_ge(ln6, LN_D * t + 3)
                nc.scalar.activation(stat[:, 0, 14:15], stat[:, 0, 13:14], ACT.Sqrt, bias=eps[:]).then_inc(std6, 1)

            def copy_x1t(t):
                act.wait_ge(rt_t1, t + 1)
                nc.scalar.activation(x1t[:], tiles(4), ACT.Copy).then_inc(rt_c, 1)

            def split_wo(k):
                act.wait_ge(wo_in[k % 4], 16 * (k // 4 + 1))
                nc.scalar.activation(wo_hi[:, k, :], wo_raw[:, k % 4, :], ACT.Copy).then_inc(wo_h, 1)

            act.wait_ge(used5, NBR * KT * RING5 + RING5 - 1)
            for k in range(4):
                split_wo(k)
            act.wait_ge(merge_ok, NBR * KT + 1)
            split_ms(0)
            for k in range(4, KT):
                split_wo(k)
            def copy_logits(t):
                act.wait_ge(rt_m, t + 1)
                nc.scalar.activation(lg_t[:], ps[0:NE, 7, 0:P], ACT.Copy).then_inc(rt_lc, 1)

            act.wait_ge(y_mm, 1)
            split_ms(1)
            norm6(0)
            with nc.scalar.Fori(1, TT - 1) as t:
                copy_x1t(t - 1)
                act.wait_ge(y_mm, t + 1)
                split_ms(t + 1)
                norm6(t)
                copy_logits(t - 1)
            copy_x1t(TT - 2)
            norm6(TT - 1)
            copy_logits(TT - 2)
            copy_x1t(TT - 1)
            copy_logits(TT - 1)
            act.wait_ge(r_exp, 1)
            nc.scalar.activation(prb[:], rt_t[:], ACT.Exp).then_inc(r_exp, 1)

            def split_first(s):
                act.wait_ge(first_in[s], 32)
                act.wait_ge(e_used, s + 1)
                nc.scalar.activation(e_hi[:, s % RSPL, :], e_first[:, s, :], ACT.Copy).then_inc(e_h, 1)

            def split(b, s):
                act.wait_ge(eraw_in[s], 16 * b)
                act.wait_ge(e_used, UPT + (b - 1) * XT + s + 1)
                nc.scalar.activation(e_hi[:, (UPT + s) % RSPL, :], e_raw[:, s, :], ACT.Copy).then_inc(e_h, 1)

            def split_x(b):
                act.wait_ge(tx_ok, b + 2)
                nc.scalar.activation(xe_hi[:], tiles(4), ACT.Copy).then_inc(xe_h, 1)

            def silu(b, n_up):
                act.wait_ge(e_used, n_up + RSPL)
                nc.scalar.activation(sil[:], ps[:, 1, :], ACT.Silu).then_inc(sil_ok, 1)

            def split_h(b):
                act.wait_ge(th_ok, b + 1)
                nc.scalar.activation(ht_hi[:], tiles(6, 1), ACT.Copy).then_inc(ht_h, 1)

            def result(b1, extra=0):
                act.wait_ge(e_used, UPT + b1 * XT + RSPL - extra)
                if not isinstance(b1, int):
                    act.wait_ge(ye_out, 16 * (b1 - 1))
                nc.scalar.activation(ye[:], flat(2), ACT.Copy, scale=gate_tab[:, bass.ds(b1 - 1, 1)]).then_inc(ye_ok, 1)

            def step(b):
                for s in range(XT):
                    split(b, s)
                    if s == 3 and (not isinstance(b, int) or b > 1):
                        result(b - 1)
                    if s == 7:
                        split_h(b - 1)
                silu(b, UPT + (b - 1) * XT + UPT)
                split_x(b + 1)

            for s in range(4):
                split_first(s)
            act.wait_ge(r_done, 1)
            tail = nc.scalar.value_load(tail_i[0:1, 0:1], min_val=NE - 3, max_val=NBLK - 3)
            split_x(0)
            for s in range(4, UPT):
                split_first(s)
            silu(0, UPT)
            split_x(1)
            step(1)
            step(2)
            with nc.scalar.Fori(3, tail + 3) as b:
                step(b)
            for s in range(DNT):
                split(tail + 3, s)
            result(tail + 2)
            split_h(tail + 2)
            result(tail + 3, UPT)
            for t in range(TT):
                st = stat[:, t % 2, :]
                act.wait_ge(ln9, LN_D * t + 3)
                nc.scalar.activation(st[:, 14:15], st[:, 13:14], ACT.Sqrt, bias=eps[:]).then_inc(std9, 1)

        @block.vector
        def _(dve):
            def col(row, j):
                return cols[:].rearrange("p r j -> p (r j)")[:, bass.ds(j + row * CT, 1)]

            class Chain:
                def __init__(self, s, start=0):
                    self.s, self.start, self.n = s, start, 0

                def __call__(self, ins):
                    ins.then_inc(self.s, 1)
                    self.wait()

                def wait(self):
                    self.n += 1
                    dve.wait_ge(self.s, self.start + self.n)

            dve.sem_inc(lo_ok, RING)
            dve.sem_inc(evac[1], 1)
            dve.sem_inc(v_l, 1)
            dve.sem_inc(sc_out, 16)
            dve.sem_inc(pt_l, 1)
            dve.sem_inc(lo5, RING5)
            dve.sem_inc(merge_ok, 1)
            dve.sem_inc(y1_ok, 1)
            dve.sem_inc(lg_ok, 1)
            dve.sem_inc(e_l, RRAW)
            for t in range(TT):
                dve.wait_ge(xt_h, t + 1)
                cut = xt_hi[:, :, t * P:(t + 1) * P]
                nc.vector.tensor_tensor(xt_lo[:, :, t * P:(t + 1) * P], tiles((t % 2) * 2), cut, ALU.subtract).then_inc(xt_l, 1)
            dve.wait_ge(wf_h, 1)
            nc.vector.tensor_tensor(wf_lo[:], wf_raw[:], wf_hi[:], ALU.subtract).then_inc(wf_l, 1)
            dve.wait_ge(cols_t, 1)
            nc.vector.tensor_copy(cols[:], ps[:, 4, 0:CT * ROWS].rearrange("p (j r) -> p r j", j=CT)).then_inc(cols_ok, 1)
            dve.wait_ge(cols_ok, 1)
            dve.wait_ge(pads, 2)

            def take_out(i, tile, link):
                kind, b = KINDS[tile], 2 * (tile % 2)
                if kind not in "ahb":
                    return
                dve.wait_ge(w_used, i * NCH + 2 * tile + 2 + RING)
                if kind == "a":
                    dve.wait_ge(evac[0], i * 4 + 2)
                    nc.vector.tensor_tensor(upad[:, CTAPS - 1:], flat(b), sg[:], ALU.mult).then_inc(evac[tile % 2], 1)
                    dve.wait_ge(evac[1], i * 4 + 2)
                elif kind == "h":
                    dve.wait_ge(evac[0], i * 4 + 3)
                    nc.vector.tensor_tensor(hpad[:, STAPS - 1:], flat(b), cbuf[:], ALU.mult).then_inc(evac[tile % 2], 1)
                    dve.wait_ge(evac[1], i * 4 + 3)
                    link(nc.vector.tensor_scalar(scacc[:], hpad[:, 0:SEQ], col(ROW_SCW, i), None, ALU.mult))
                    for j in range(1, STAPS):
                        link(nc.vector.scalar_tensor_tensor(scacc[:], hpad[:, j:j + SEQ], col(ROW_SCW + j, i), scacc[:], ALU.mult, ALU.add))
                else:
                    dve.wait_ge(sc_out, 16 * i + 16)
                    nc.vector.tensor_tensor(sc1[:], flat(b), scacc[:], ALU.mult).then_inc(evac[tile % 2], 1)

            with nc.vector.Fori(0, CT) as i:
                link = Chain(conv_chain, i * CONV_LINKS)
                dst = conv[:, bass.ds(i, 1), :].rearrange("p a n -> p (a n)")
                taps = list(range(CTAPS))
                for c in range(NCH):
                    dve.wait_ge(hi_ok, i * NCH + c + 1)
                    nc.vector.tensor_tensor(w_lo[:, c % RING], w_raw[:, c % RING], w_hi[:, c % RING], ALU.subtract).then_inc(lo_ok, 1)
                    if c >= 3 and c % 2 == 1:
                        take_out(i, (c - 3) // 2, link)
                    if c >= 5:
                        for j in taps[:3]:
                            if j == 0:
                                link(nc.vector.tensor_scalar(dst, upad[:, 0:SEQ], col(ROW_CONVW, i), col(ROW_CONVB, i), ALU.mult, ALU.add))
                            else:
                                link(nc.vector.scalar_tensor_tensor(dst, upad[:, j:j + SEQ], col(ROW_CONVW + j, i), dst, ALU.mult, ALU.add))
                        taps = taps[3:]
                assert not taps and link.n == CONV_LINKS
            link = Chain(ln_dve)
            for t in range(TT):
                dve.wait_ge(ln_t, t + 1)
                nc.vector.bn_stats(stat3[:, t, 0:6], ps[:, bank3(t), :]).then_inc(ln_stats, 1)
            dve.wait_ge(ln_stats, TT)
            for t in range(TT):
                nc.vector.bn_aggr(aggr3[:, t, :], stat3[:, t, 0:6]).then_inc(ln_stats, 1)
            dve.wait_ge(std3, 1)
            link(nc.vector.reciprocal(rstd3[:], rstd3[:]))
            for t in range(TT):
                if t >= 2:
                    dve.wait_ge(ln_t2, t - 1)
                nc.vector.tensor_scalar(yln[:, t % 2, :], ps[:, bank3(t), :], aggr3[:, t, 0:1], rstd3[:, t:t + 1],
                                        ALU.subtract, ALU.mult).then_inc(ln_dve, 1)
            link = Chain(f_dve)
            dve.wait_ge(f_act, 4)
            link(nc.vector.scalar_tensor_tensor(fz[:], fz[:], 0.0, fe[:], ALU.min, ALU.subtract))
            link(nc.vector.memset(fe[:], 1.0))
            link(nc.vector.tensor_tensor_scan(fc[:], fe[:], fz[:], 0.0, ALU.mult, ALU.add))
            link(nc.vector.tensor_scalar(fz[:], fc[:], -1.0, None, ALU.mult))
            def maximum(i, g):
                dve.wait_ge(s_ok, i * 2 * TT + g + 1)
                nc.vector.tensor_reduce(rmax[:, g % 2:g % 2 + 1], flat(2 * (g % 2))[:, 0:nkeys(g % TT) * P], AX.X, ALU.max,
                                        negate=True).then_inc(max_ok, 1)

            def normalize(i, g):
                n = i * 2 * TT + g
                dve.wait_ge(exp_ok, n + 1)
                nc.vector.reciprocal(rinv[:, g % 2:g % 2 + 1], rsum[:, g % 2:g % 2 + 1]).then_inc(inv_ok, 1)
                dve.wait_ge(inv_ok, n + 1)
                cut = prob[:, g % 2, 0:nkeys(g % TT) * P]
                nc.vector.tensor_scalar(cut, cut, rinv[:, g % 2:g % 2 + 1], None, ALU.mult).then_inc(norm_ok, 1)

            def split_pt(i, t):
                r = t % TT
                dve.wait_ge(pt_h, i * 2 * TT + t + 1)
                cut = (slice(None), t // 2 % 2, slice(0, nkeys(r)), slice((r % 2) * P, (r % 2 + 1) * P))
                nc.vector.tensor_tensor(pt_lo[cut], tiles(4)[:, 0:nkeys(r), :], pt_hi[cut], ALU.subtract).then_inc(pt_l, 1)

            def split_v(i, half):
                dve.wait_ge(v_h, 2 * i + half + 1)
                cut = (slice(None), slice(half * KC, (half + 1) * KC))
                nc.vector.tensor_tensor(v_lo[cut], tiles(7, 1), v_hi[cut], ALU.subtract).then_inc(v_l, 1)

            def dve_step(i, g):
                for lag, what in ((0, maximum), (1, normalize), (2, split_pt)):
                    j, t = (i, g - lag) if g >= lag else (i - 1, g - lag + 2 * TT)
                    if not (isinstance(j, int) and j < 0):
                        what(j, t)
                if g in (2, 3):
                    split_v(i, g - 2)

            for g in range(2 * TT):
                dve_step(0, g)
            with nc.vector.Fori(1, HEADS // 2) as i:
                for g in range(2 * TT):
                    dve_step(i, g)
            normalize(HEADS // 2 - 1, 2 * TT - 1)
            split_pt(HEADS // 2 - 1, 2 * TT - 2)
            split_pt(HEADS // 2 - 1, 2 * TT - 1)
            def split_wo(k):
                dve.wait_ge(wo_h, k + 1)
                nc.vector.tensor_tensor(wo_lo[:, k, :], wo_raw[:, k % 4, :], wo_hi[:, k, :], ALU.subtract).then_inc(wo_l, 1)

            def split5(m, i, c):
                dve.wait_ge(hi5, (m * KT + i) * RING5 + c + 1)
                nc.vector.tensor_tensor(w_lo[:, c], w_raw[:, c], w_hi[:, c], ALU.subtract).then_inc(lo5, 1)

            def merge(m, i):
                dve.wait_ge(used5, (m * KT + i + 1) * RING5 + RING5)
                dve.wait_ge(gate_ok, m * KT + i + 2)
                dst = merged[:, bass.ds(i, 1), :].rearrange("p a n -> p (a n)")
                if m == 0:
                    nc.vector.tensor_tensor(dst, flat(2), gate_s[:], ALU.mult).then_inc(merge_ok, 1)
                else:
                    nc.vector.tensor_tensor(gate_s[:], flat(2), gate_s[:], ALU.mult).then_inc(merge_chain, 1)
                    dve.wait_ge(merge_chain, (m - 1) * KT + i + 1)
                    nc.vector.tensor_tensor(dst, dst, gate_s[:], ALU.add).then_inc(merge_ok, 1)

            for m in range(NBR):
                split5(m, 0, 0)
                split5(m, 0, 1)
                if m > 0:
                    merge(m - 1, KT - 1)
                src = (qkv[:, 0:CT, :], br_raw[:], br_raw[:])[m]
                for k in range(CT):
                    dve.wait_ge(br_h, m * CT + k + 1)
                    nc.vector.tensor_tensor(br_lo[:, k], src[:, k], br_hi[:, k], ALU.subtract).then_inc(br_l, 1)
                split5(m, 0, 2)
                with nc.vector.Fori(1, KT) as i:
                    split5(m, i, 0)
                    split5(m, i, 1)
                    merge(m, i - 1)
                    split5(m, i, 2)
            for k in range(4):
                split_wo(k)
            merge(NBR - 1, KT - 1)

            def split_ms(t):
                dve.wait_ge(ms_h, t + 1)
                for k in (0, KC):
                    nc.vector.tensor_tensor(ms_lo[:, k:k + KC], merged[:, k:k + KC, bass.ds(t * P, P)], ms_hi[:, k:k + KC],
                                            ALU.subtract).then_inc(ms_l, 1)

            def centre(src, st, gain, link, std, count):
                link(nc.vector.bn_stats(st[:, 0:6], src[:, 0:HALF]))
                nc.vector.bn_stats(st[:, 6:12], src[:, HALF:D]).then_inc(link.s, 1)
                link.wait()
                dve.sem_inc(passed_dve, 1)
                link(nc.vector.bn_aggr(st[:, 12:14], st[:, 0:12]))
                link(nc.vector.scalar_tensor_tensor(src, src, st[:, 12:13], gain, ALU.subtract, ALU.mult))
                dve.wait_ge(std, count)
                link(nc.vector.reciprocal(st[:, 14:15], st[:, 14:15]))

            def residual(t):
                dve.wait_ge(y_mm, t + 1)
                dve.wait_ge(xres_in, 16 * (t + 1))
                nc.vector.scalar_tensor_tensor(y1[:], x_res[:], ALPHA, flat(0), ALU.mult, ALU.add).then_inc(y1_ok, 1)
                dve.wait_ge(y1_ok, t + 2)

            def norm6(t, x1_used):
                link = Chain(ln6, LN_D * t)
                centre(y1[:], stat[:, 0, :], lng1[:], link, std6, t + 1)
                assert link.n == LN_D
                if x1_used:
                    dve.wait_ge(rt_t1, t)
                    dve.wait_ge(x1_out, 16 * t)
                nc.vector.scalar_tensor_tensor(x1[:], y1[:], stat[:, 0, 14:15], lnb1[:], ALU.mult, ALU.add).then_inc(x1_ok, 1)

            def take_logits(t):
                dve.wait_ge(rt_mm, t + 1)
                nc.vector.tensor_tensor(logits[:, bass.ds(t, 1), :].rearrange("p a n -> p (a n)"), ps[:, 6, 0:NE],
                                        b_rt[:], ALU.add).then_inc(lg_ok, 1)

            split_ms(0)
            for k in range(4, KT):
                split_wo(k)
            dve.wait_ge(par6_in, 64)
            residual(0)
            split_ms(1)
            norm6(0, False)
            residual(1)
            split_ms(2)
            norm6(1, True)
            with nc.vector.Fori(2, TT - 1) as t:
                take_logits(t - 2)
                residual(t)
                split_ms(t + 1)
                norm6(t, True)
            residual(TT - 1)
            take_logits(TT - 3)
            norm6(TT - 1, True)
            take_logits(TT - 2)
            take_logits(TT - 1)

            link = Chain(r_chain)
            dve.wait_ge(lg_ok, TT + 1)
            dve.wait_ge(r_const, 10)

            def wide(v, n):
                return v.unsqueeze(len(v.shape)).to_broadcast(list(v.shape) + [n])

            def groups(v):
                return v[:].rearrange("p t (g e) -> p t g e", e=EPG)

            V = nc.vector
            tmax, tsum, trec, v1, v2, vs, vr = (byt[:, j, :] for j in range(7))
            m1, m2, first, score, ohg, gsc = (grp[:, j] for j in range(6))
            link(V.tensor_reduce(tmax, logits[:], AX.X, ALU.max))
            link(V.tensor_tensor(rt_t[:], logits[:], wide(tmax, NE), ALU.subtract))
            dve.sem_inc(r_exp, 1)
            dve.wait_ge(r_exp, 2)
            link(V.tensor_reduce(tsum, prb[:], AX.X, ALU.add))
            link(V.reciprocal(trec, tsum))
            link(V.tensor_tensor(prb[:], prb[:], wide(trec, NE), ALU.mult))
            link(V.tensor_reduce(m1, groups(prb), AX.X, ALU.max))
            link(V.tensor_tensor(groups(rt_t), groups(prb), wide(m1, EPG), ALU.is_equal))
            link(V.tensor_tensor(groups(rt_t), groups(rt_t), kneg[:], ALU.mult))
            link(V.tensor_reduce(first, groups(rt_t), AX.X, ALU.max))
            link(V.tensor_tensor(groups(oh1), groups(rt_t), wide(first, EPG), ALU.is_equal))
            link(V.scalar_tensor_tensor(p2[:], oh1[:], -2.0, prb[:], ALU.mult, ALU.add))
            link(V.tensor_reduce(m2, groups(p2), AX.X, ALU.max))
            link(V.tensor_tensor(groups(rt_t), groups(p2), wide(m2, EPG), ALU.is_equal))
            link(V.tensor_tensor(groups(rt_t), groups(rt_t), kneg[:], ALU.mult))
            link(V.tensor_reduce(first, groups(rt_t), AX.X, ALU.max))
            link(V.tensor_tensor(groups(oh2), groups(rt_t), wide(first, EPG), ALU.is_equal))
            link(V.tensor_tensor(score, m1, m2, ALU.add))
            link(V.tensor_reduce(tmax, score, AX.X, ALU.max))
            link(V.tensor_tensor(gsc, score, wide(tmax, NG), ALU.is_equal))
            link(V.tensor_tensor(gsc, gsc, gneg[:], ALU.mult))
            link(V.tensor_reduce(tmax, gsc, AX.X, ALU.max))
            link(V.tensor_tensor(ohg, gsc, wide(tmax, NG), ALU.is_equal))
            link(V.tensor_tensor(groups(oh1), groups(oh1), wide(ohg, EPG), ALU.mult))
            link(V.tensor_tensor(groups(oh2), groups(oh2), wide(ohg, EPG), ALU.mult))
            link(V.tensor_tensor(sel_b[:], oh1[:], oh2[:], ALU.add))
            dve.sem_inc(r_sel, 1)
            link(V.tensor_tensor(m1, m1, ohg, ALU.mult))
            link(V.tensor_reduce(v1, m1, AX.X, ALU.add))
            link(V.tensor_tensor(m2, m2, ohg, ALU.mult))
            link(V.tensor_reduce(v2, m2, AX.X, ALU.add))
            link(V.tensor_tensor(vs, v1, v2, ALU.add))
            link(V.reciprocal(vr, vs))
            for k, v in enumerate((v1, v2)):
                link(V.tensor_tensor(gates[:, k, :], v, vr, ALU.mult))
            dve.wait_ge(r_cnt, 1)
            before, per_tile = (ps[:, b, 0:TT * NE].rearrange("p (t e) -> p t e", e=NE) for b in (0, 1))
            link(V.memset(tcum[:, 0, :], 0.0))
            for t in range(1, TT):
                link(V.tensor_tensor(tcum[:, t, :], tcum[:, t - 1, :], per_tile[:, t - 1, :], ALU.add))
            count, extra, upto, diff, start, inc32, lowb, eb = (ev[:, j, :] for j in range(8))
            link(V.tensor_tensor(count, tcum[:, TT - 1, :], per_tile[:, TT - 1, :], ALU.add))
            link(V.tensor_tensor(gt[:], wide(count, TT - 1), thr[:], ALU.is_gt))
            link(V.tensor_reduce(extra, gt[:], AX.X, ALU.add))
            link(V.tensor_tensor_scan(upto, ones_e[:], extra, 0.0, ALU.mult, ALU.add))
            link(V.tensor_scalar(last_i[:], upto[:, NE - 1:NE], float(NE - 1), None, ALU.add))
            link(V.tensor_scalar(tail_i[:], upto[:, NE - 1:NE], float(NE - 3), None, ALU.add))
            link(V.tensor_tensor(start, upto, extra, ALU.subtract))
            link(V.tensor_scalar(start, start, float(NE - 1), None, ALU.add))
            link(V.tensor_tensor(diff, start, biota[:, 0:NE], ALU.subtract))
            link(V.tensor_scalar(diff, diff, float(P), None, ALU.mult))
            link(V.tensor_scalar(start, biota[:, 0:NE], float(P), None, ALU.mult))
            link(V.tensor_tensor(dest[:], before, tcum[:], ALU.add))

            def by_tile(v):
                return v.unsqueeze(1).to_broadcast([P, TT, NE])

            link(V.scalar_tensor_tensor(rt_t[:], dest[:], float(P), by_tile(diff), ALU.is_ge, ALU.mult))
            link(V.tensor_tensor(dest[:], dest[:], by_tile(start), ALU.add))
            link(V.tensor_tensor(dest[:], dest[:], rt_t[:], ALU.add))
            for k, oh in enumerate((oh1, oh2)):
                link(V.tensor_tensor(rt_u[:], dest[:], oh[:], ALU.mult))
                link(V.tensor_reduce(dest_f[:, k, :], rt_u[:], AX.X, ALU.add))
            link(V.tensor_copy(dest_i[:], dest_f[:]))
            link(V.tensor_scalar(blk_i[:], dest_i[:], P.bit_length() - 1, None, ALU.arith_shift_right))
            link(V.tensor_copy(blk_f[:], blk_i[:]))
            link(V.scalar_tensor_tensor(rank_f[:], blk_f[:], -float(P), dest_f[:], ALU.mult, ALU.add))
            for k in range(TOPK):
                link(V.tensor_tensor(by_rank[:, k], iota_p[:].unsqueeze(1).to_broadcast([P, TT, P]), wide(rank_f[:, k, :], P), ALU.is_equal))
                link(V.tensor_tensor(by_blk[:, k], biota[:].unsqueeze(1).to_broadcast([P, TT, NB1]), wide(blk_f[:, k, :], NB1), ALU.is_equal))
                for c, v in enumerate((tokm[:], rowm[:, k, :], gates[:, k, :])):
                    link(V.tensor_tensor(vals[:, k, :, c, :], by_blk[:, k], wide(v, NB1), ALU.mult))
            dve.sem_inc(r_vals, 1)
            link(V.tensor_scalar(inc32, upto, float(NE), None, ALU.add))
            dve.wait_ge(x1_out, 16 * TT)
            link(V.tensor_tensor(bmap[:], wide(biota[:, 0:NBLK], NE), inc32.unsqueeze(1).to_broadcast([P, NBLK, NE]), ALU.is_ge))
            link(V.tensor_reduce(rt_u[:].rearrange("p t e -> p (t e)")[:, 0:NBLK], bmap[:], AX.X, ALU.add))
            link(V.scalar_tensor_tensor(rt_t[:].rearrange("p t e -> p (t e)")[:, 0:NBLK], biota[:, 0:NBLK], float(NE), biota[:, 0:NBLK], ALU.is_lt, ALU.mult))
            link(V.tensor_tensor(rt_u[:].rearrange("p t e -> p (t e)")[:, 0:NBLK], rt_u[:].rearrange("p t e -> p (t e)")[:, 0:NBLK],
                                 rt_t[:].rearrange("p t e -> p (t e)")[:, 0:NBLK], ALU.add))
            link(V.tensor_scalar(expert_i[:], rt_u[:].rearrange("p t e -> p (t e)")[:, 0:NBLK], float(NE - 1), None, ALU.min))
            dve.wait_ge(r_tab, 1)
            tab = ps[:, 7, 0:3 * NB1].rearrange("p (c b) -> p c b", c=3)
            link(V.tensor_scalar(tok_tab[:], tab[:, 0, :], float(NO_TOK), None, ALU.add))
            link(V.tensor_scalar(row_tab[:], tab[:, 1, :], float(NO_ROW), None, ALU.add))
            link(V.tensor_copy(gate_tab[:], tab[:, 2, :]))
            dve.sem_inc(r_done, 1)

            def split_first(s):
                dve.wait_ge(e_h, s + 1)
                nc.vector.tensor_tensor(e_lo[:, s % RSPL, :], e_first[:, s, :], e_hi[:, s % RSPL, :], ALU.subtract).then_inc(e_all, 1)

            def split(n, s):
                dve.wait_ge(e_h, UPT + n + 1)
                sp_ = (UPT + s) % RSPL
                nc.vector.tensor_tensor(e_lo[:, sp_, :], e_raw[:, s, :], e_hi[:, sp_, :], ALU.subtract).then_inc(e_all, 1)
                dve.wait_ge(e_all, UPT + n + 1)
                dve.sem_inc(e_l, 1)

            def split_x(b):
                dve.wait_ge(xe_h, b + 1)
                nc.vector.tensor_tensor(xe_lo[:], tiles(4), xe_hi[:], ALU.subtract).then_inc(xe_l, 1)

            def hidden(b):
                dve.wait_ge(sil_ok, b + 1)
                nc.vector.tensor_tensor(hid[:], ps[:, 0, :], sil[:], ALU.mult).then_inc(hid_ok, 1)

            def split_h(b):
                dve.wait_ge(ht_h, b + 1)
                nc.vector.tensor_tensor(ht_lo[:], tiles(6, 1), ht_hi[:], ALU.subtract).then_inc(ht_l, 1)

            for s in range(4):
                split_first(s)
            last_b = nc.vector.value_load(last_i[0:1, 0:1], min_val=NE - 1, max_val=NBLK - 1)
            split_x(0)
            for s in range(4, UPT):
                split_first(s)
            hidden(0)
            split_x(1)
            with nc.vector.Fori(1, last_b + 1) as b:
                for s in range(XT):
                    split((b - 1) * XT + s, s)
                    if s == 7:
                        split_h(b - 1)
                hidden(b)
                split_x(b + 1)
            for s in range(DNT):
                split(last_b * XT + s, s)
            split_h(last_b)
            dve.wait_ge(par9_in, 32)
            for t in range(TT):
                dve.wait_ge(add2[t], 16)
                centre(comb[:, t, :], stat[:, t % 2, :], lng2[:], Chain(ln9, LN_D * t), std9, t + 1)
                if t >= 2:
                    dve.wait_ge(out_dma[t % 2], 16 * (t // 2))
                nc.vector.scalar_tensor_tensor(zout[:, t % 2, :], comb[:, t, :], stat[:, t % 2, 14:15], lnb2[:],
                                               ALU.mult, ALU.add).then_inc(out_ok, 1)


_INS = ["x", "w_in", "b_forget", "conv_w", "conv_b", "conv_ln_g", "conv_ln_b", "sc_w", "w_branch", "w_gate",
        "b_gate", "w_out", "ln1_g", "ln1_b", "w_up", "w_down", "ln2_g", "ln2_b", "w_router", "b_router"]


def kernel(**inputs):
    import concourse.bacc as bacc
    from concourse.bass_utils import run_bass_kernel_spmd

    nc = bacc.Bacc("TRN2", target_bir_lowering=False, num_devices=1)
    arrays = {"in_" + n: np.ascontiguousarray(inputs[n]) for n in _INS}
    args = [nc.dram_tensor(n, a.shape, mybir.dt.from_np(a.dtype), kind="ExternalInput").ap() for n, a in arrays.items()]
    out = nc.dram_tensor("out_0", (1, SEQ, D), FP32, kind="ExternalOutput").ap()
    program(nc, *args, out)
    return run_bass_kernel_spmd(nc, [arrays], core_ids=[0]).results[0]["out_0"]
```
